# Optimizing a Trainium2 kernel written in Bass

```python
import jax, jax.numpy as jnp
from jax import lax
import numpy as np

D_MODEL = 1024
BATCH = 1
SEQ = 256
DEPTH = 2
DEC_BATCH = 8
DEC_SEQ = 8
PAST_LEN = 2048
PAGE_SIZE = 128

MIX_WIDTH = D_MODEL
GLA_HEADS = 4
GLA_WIDTH = MIX_WIDTH // 2
GLA_DV = GLA_WIDTH // GLA_HEADS
GLA_DK = GLA_DV // 2
GLA_KW = GLA_HEADS * GLA_DK
GLA_RANK = 16
GLA_GATE_NORM = 16.0
GDN_HEADS = 4
GDN_WIDTH = MIX_WIDTH - GLA_WIDTH
GDN_DK = GDN_WIDTH // GDN_HEADS
GDN_DV = GDN_DK
CONV_W = 4
CHUNK = 64
PEER_HEADS = 8
PEER_QDIM = 256
PEER_HALF = PEER_QDIM // 2
N_KEYS = 128
N_EXPERTS = N_KEYS * N_KEYS
PEER_TOPK = 16
PEER_BLOCK = 256
PLE_DIM = 256
EPS = 1e-6
SPLIT_SIZES = (GLA_KW, GLA_KW, GLA_WIDTH, GLA_WIDTH, GLA_RANK, 3 * GDN_WIDTH, GDN_WIDTH, GDN_HEADS, GDN_HEADS)
IN_WIDTH = sum(SPLIT_SIZES)

kernel_name = 'hybrid_gla_gdn_peer_step'

def _rmsnorm(x, g):
    xf = x.astype(jnp.float32)
    y = xf * lax.rsqrt(jnp.mean(xf * xf, axis=-1, keepdims=True) + EPS)
    return (y * g.astype(jnp.float32)).astype(x.dtype)

def _l2norm(x):
    return x * lax.rsqrt(jnp.sum(x * x, axis=-1, keepdims=True) + EPS)

def _split_cols(x, sizes):
    out, off = [], 0
    for s in sizes:
        out.append(x[..., off:off + s])
        off += s
    return out

def _chunk_len(L):
    return CHUNK if L >= CHUNK else L

def _to_chunks(x, C):
    B, L = x.shape[0], x.shape[1]
    n_pad = (-L) % C
    x = jnp.pad(x, [(0, 0), (0, n_pad)] + [(0, 0)] * (x.ndim - 2))
    x = x.reshape((B, (L + n_pad) // C, C) + x.shape[2:])
    return jnp.moveaxis(x, 1, 0)

def _from_chunks(y, L):
    nc, B, C = y.shape[0], y.shape[1], y.shape[2]
    y = jnp.moveaxis(y, 0, 1).reshape((B, nc * C) + y.shape[3:])
    return y[:, :L]

def _gla_recurrence(q, k, v, gk, s0):
    L = q.shape[1]
    C = _chunk_len(L)
    incl = jnp.tril(jnp.ones((C, C), dtype=bool))[None, :, :, None, None]

    def step(S, inp):
        qc, kc, vc, gc = inp
        b = jnp.cumsum(gc, axis=1)
        rel = b[:, :, None] - b[:, None, :]
        decay = jnp.where(incl, jnp.exp(jnp.where(incl, rel, 0.0)), 0.0)
        att = jnp.einsum('bthk,bshk,btshk->bhts', qc, kc, decay)
        o = jnp.einsum('bhts,bshv->bthv', att, vc) + jnp.einsum('bthk,bhkv->bthv', qc * jnp.exp(b), S)
        b_last = b[:, -1]
        S = jnp.exp(b_last)[..., None] * S + jnp.einsum('bshk,bshv->bhkv', kc * jnp.exp(b_last[:, None] - b), vc)
        return S, o

    S, o = lax.scan(step, s0, (_to_chunks(q, C), _to_chunks(k, C), _to_chunks(v, C), _to_chunks(gk, C)))
    return _from_chunks(o, L), S

def _gdn_recurrence(q, k, v, g, beta, s0):
    L = q.shape[1]
    C = _chunk_len(L)
    incl = jnp.tril(jnp.ones((C, C), dtype=bool))
    strict = jnp.tril(jnp.ones((C, C), dtype=bool), k=-1)
    eye = jnp.eye(C, dtype=jnp.float32)

    def step(S, inp):
        qc, kc, vc, gc, bc = inp
        b = jnp.cumsum(gc, axis=1)
        bh = jnp.moveaxis(b, 1, 2)
        rel = bh[..., :, None] - bh[..., None, :]
        decay = jnp.where(incl, jnp.exp(jnp.where(incl, rel, 0.0)), 0.0)
        kb = kc * bc[..., None]
        lower = jnp.where(strict, jnp.einsum('bthk,bshk->bhts', kb, kc) * decay, 0.0)
        rhs = jnp.concatenate([vc * bc[..., None], kb * jnp.exp(b)[..., None]], axis=-1)
        rhs = jnp.moveaxis(rhs, 1, 2)
        sol = lax.linalg.triangular_solve(eye + lower, rhs, left_side=True, lower=True, unit_diagonal=True)
        u, w = sol[..., :GDN_DV], sol[..., GDN_DV:]
        v_new = u - jnp.einsum('bhtk,bhkv->bhtv', w, S)
        qk = jnp.einsum('bthk,bshk->bhts', qc, kc) * decay
        o = jnp.einsum('bthk,bhkv->bthv', qc * jnp.exp(b)[..., None], S) + jnp.einsum('bhts,bhsv->bthv', qk, v_new)
        b_last = b[:, -1]
        S = jnp.exp(b_last)[..., None, None] * S + jnp.einsum('bshk,bhsv->bhkv', kc * jnp.exp(b_last[:, None] - b)[..., None], v_new)
        return S, o

    xs = (_to_chunks(q, C), _to_chunks(k, C), _to_chunks(v, C), _to_chunks(g, C), _to_chunks(beta, C))
    S, o = lax.scan(step, s0, xs)
    return _from_chunks(o, L), S

def _mixer(a, w_in, w_gla_up, b_gla_gate, gla_norm, conv_w, gdn_a_log, gdn_dt_bias, gdn_norm, w_out, s_gla, s_gdn, conv_buf):
    f32 = jnp.float32
    B, L, _ = a.shape
    q1, k1, v1, r1, lr, qkv2, z2, b2, a2 = _split_cols(a @ w_in, SPLIT_SIZES)
    gk = jax.nn.log_sigmoid((lr @ w_gla_up + b_gla_gate).astype(f32)) / GLA_GATE_NORM
    q1 = q1.astype(f32).reshape(B, L, GLA_HEADS, GLA_DK) * (GLA_DK ** -0.5)
    k1 = k1.astype(f32).reshape(B, L, GLA_HEADS, GLA_DK)
    v1 = v1.astype(f32).reshape(B, L, GLA_HEADS, GLA_DV)
    gk = gk.reshape(B, L, GLA_HEADS, GLA_DK)
    o1, s_gla_new = _gla_recurrence(q1, k1, v1, gk, s_gla.astype(f32))
    o1 = _rmsnorm(o1, gla_norm).reshape(B, L, GLA_WIDTH) * jax.nn.silu(r1.astype(f32))
    xx = jnp.concatenate([conv_buf.astype(qkv2.dtype), qkv2], axis=1)
    conv = xx[:, 0:L] * conv_w[0]
    for j in range(1, CONV_W):
        conv = conv + xx[:, j:j + L] * conv_w[j]
    conv_new = xx[:, L:]
    q2, k2, v2 = _split_cols(jax.nn.silu(conv.astype(f32)), (GDN_WIDTH, GDN_WIDTH, GDN_WIDTH))
    q2 = _l2norm(q2.reshape(B, L, GDN_HEADS, GDN_DK)) * (GDN_DK ** -0.5)
    k2 = _l2norm(k2.reshape(B, L, GDN_HEADS, GDN_DK))
    v2 = v2.reshape(B, L, GDN_HEADS, GDN_DV)
    beta = jax.nn.sigmoid(b2.astype(f32))
    g = -jnp.exp(gdn_a_log.astype(f32)) * jax.nn.softplus(a2.astype(f32) + gdn_dt_bias.astype(f32))
    o2, s_gdn_new = _gdn_recurrence(q2, k2, v2, g, beta, s_gdn.astype(f32))
    o2 = (_rmsnorm(o2, gdn_norm) * jax.nn.silu(z2.astype(f32).reshape(B, L, GDN_HEADS, GDN_DV))).reshape(B, L, GDN_WIDTH)
    o = jnp.concatenate([o1, o2], axis=-1).astype(a.dtype) @ w_out
    return o, s_gla_new, s_gdn_new, conv_new

def _peer(a, w_pq, sub_keys, u_tab, v_tab):
    B, L, D = a.shape
    n = B * L
    nb = -(-n // PEER_BLOCK)
    t = jnp.pad(a.reshape(n, D), ((0, nb * PEER_BLOCK - n), (0, 0)))
    blocks = t.reshape(nb, PEER_BLOCK, D)
    keys = sub_keys.astype(jnp.float32)

    def block_fn(xb):
        q = (xb @ w_pq).astype(jnp.float32).reshape(PEER_BLOCK, PEER_HEADS, 2, PEER_HALF)
        s = jnp.einsum('thcd,hcnd->thcn', q, keys)
        sv, si = lax.top_k(s, PEER_TOPK)
        cand = sv[:, :, 0, :, None] + sv[:, :, 1, None, :]
        cand_idx = si[:, :, 0, :, None] * N_KEYS + si[:, :, 1, None, :]
        cv, ci = lax.top_k(cand.reshape(PEER_BLOCK, PEER_HEADS, PEER_TOPK * PEER_TOPK), PEER_TOPK)
        idx = jnp.take_along_axis(cand_idx.reshape(PEER_BLOCK, PEER_HEADS, PEER_TOPK * PEER_TOPK), ci, axis=-1)
        gate = jax.nn.softmax(cv, axis=-1)
        u = jnp.take(u_tab, idx, axis=0)
        hid = jax.nn.gelu(jnp.einsum('td,thkd->thk', xb, u).astype(jnp.float32), approximate=False)
        vv = jnp.take(v_tab, idx, axis=0)
        return jnp.einsum('thk,thkd->td', (gate * hid).astype(xb.dtype), vv)

    out = lax.map(block_fn, blocks).reshape(nb * PEER_BLOCK, D)[:n]
    return out.reshape(B, L, D)

def _trunk(x, p, s_gla, s_gdn, s_conv, params):
    (norm_mix, w_in, w_gla_up, b_gla_gate, gla_norm, conv_w, gdn_a_log, gdn_dt_bias, gdn_norm, w_out,
     norm_ffn, w_peer_q, peer_sub_keys, peer_u, peer_v, norm_ple, w_ple_gate, b_ple_gate, w_ple_proj, norm_final) = params
    h = x
    new_gla, new_gdn, new_conv = [], [], []
    for i in range(DEPTH):
        mix, sg, sd, sc = _mixer(_rmsnorm(h, norm_mix[i]), w_in[i], w_gla_up[i], b_gla_gate[i], gla_norm[i], conv_w[i],
                                 gdn_a_log[i], gdn_dt_bias[i], gdn_norm[i], w_out[i], s_gla[i], s_gdn[i], s_conv[i])
        h = h + mix
        h = h + _peer(_rmsnorm(h, norm_ffn[i]), w_peer_q[i], peer_sub_keys[i], peer_u[i], peer_v[i])
        gate = jax.nn.sigmoid(_rmsnorm(h, norm_ple[i]) @ w_ple_gate[i] + b_ple_gate[i])
        h = h + gate * (p[i] @ w_ple_proj[i])
        new_gla.append(sg)
        new_gdn.append(sd)
        new_conv.append(sc)
    y = _rmsnorm(h, norm_final)
    return y, jnp.stack(new_gla), jnp.stack(new_gdn), jnp.stack(new_conv)

def setup_inputs(seed: int = 0) -> dict:
    key = jax.random.key(seed)
    ks = jax.random.split(key, 32)
    f32 = jnp.float32

    def nrm(k, shape, scale):
        return jax.random.normal(k, shape, f32) * scale

    def gain(k, shape):
        return 1.0 + 0.02 * jax.random.normal(k, shape, f32)

    return {
        'x_prompt': nrm(ks[0], (BATCH, SEQ, D_MODEL), 1.0),
        'x_sample': nrm(ks[1], (DEC_BATCH, DEC_SEQ, D_MODEL), 1.0),
        'state_gla': nrm(ks[2], (DEPTH, DEC_BATCH, GLA_HEADS, GLA_DK, GLA_DV), 0.1),
        'state_gdn': nrm(ks[3], (DEPTH, DEC_BATCH, GDN_HEADS, GDN_DK, GDN_DV), 0.1),
        'state_conv': nrm(ks[4], (DEPTH, DEC_BATCH, CONV_W - 1, 3 * GDN_WIDTH), 1.0),
        'p_prompt': nrm(ks[5], (DEPTH, BATCH, SEQ, PLE_DIM), 1.0),
        'p_sample': nrm(ks[6], (DEPTH, DEC_BATCH, DEC_SEQ, PLE_DIM), 1.0),
        'norm_mix': gain(ks[7], (DEPTH, D_MODEL)),
        'w_in': nrm(ks[8], (DEPTH, D_MODEL, IN_WIDTH), D_MODEL ** -0.5),
        'w_gla_up': nrm(ks[9], (DEPTH, GLA_RANK, GLA_KW), GLA_RANK ** -0.5),
        'b_gla_gate': nrm(ks[10], (DEPTH, GLA_KW), 0.1),
        'gla_norm': gain(ks[11], (DEPTH, GLA_DV)),
        'conv_w': nrm(ks[12], (DEPTH, CONV_W, 3 * GDN_WIDTH), CONV_W ** -0.5),
        'gdn_a_log': jnp.log(jax.random.uniform(ks[13], (DEPTH, GDN_HEADS), f32, 1.0, 16.0)),
        'gdn_dt_bias': nrm(ks[14], (DEPTH, GDN_HEADS), 0.1),
        'gdn_norm': gain(ks[15], (DEPTH, GDN_DV)),
        'w_out': nrm(ks[16], (DEPTH, MIX_WIDTH, D_MODEL), 0.5 * MIX_WIDTH ** -0.5),
        'norm_ffn': gain(ks[17], (DEPTH, D_MODEL)),
        'w_peer_q': nrm(ks[18], (DEPTH, D_MODEL, PEER_HEADS * PEER_QDIM), D_MODEL ** -0.5),
        'peer_sub_keys': nrm(ks[19], (DEPTH, PEER_HEADS, 2, N_KEYS, PEER_HALF), PEER_HALF ** -0.5),
        'peer_u': nrm(ks[20], (DEPTH, N_EXPERTS, D_MODEL), D_MODEL ** -0.5),
        'peer_v': nrm(ks[21], (DEPTH, N_EXPERTS, D_MODEL), 0.5 * PEER_HEADS ** -0.5),
        'norm_ple': gain(ks[22], (DEPTH, D_MODEL)),
        'w_ple_gate': nrm(ks[23], (DEPTH, D_MODEL, D_MODEL), D_MODEL ** -0.5),
        'b_ple_gate': nrm(ks[24], (DEPTH, D_MODEL), 0.1),
        'w_ple_proj': nrm(ks[25], (DEPTH, PLE_DIM, D_MODEL), 0.5 * PLE_DIM ** -0.5),
        'norm_final': gain(ks[26], (D_MODEL,)),
    }

def reference(x_prompt, x_sample, state_gla, state_gdn, state_conv, p_prompt, p_sample,
              norm_mix, w_in, w_gla_up, b_gla_gate, gla_norm, conv_w, gdn_a_log, gdn_dt_bias, gdn_norm, w_out,
              norm_ffn, w_peer_q, peer_sub_keys, peer_u, peer_v, norm_ple, w_ple_gate, b_ple_gate, w_ple_proj, norm_final):
    params = (norm_mix, w_in, w_gla_up, b_gla_gate, gla_norm, conv_w, gdn_a_log, gdn_dt_bias, gdn_norm, w_out,
              norm_ffn, w_peer_q, peer_sub_keys, peer_u, peer_v, norm_ple, w_ple_gate, b_ple_gate, w_ple_proj, norm_final)
    B = x_prompt.shape[0]
    gla0 = jnp.zeros((DEPTH, B, GLA_HEADS, GLA_DK, GLA_DV), jnp.float32)
    gdn0 = jnp.zeros((DEPTH, B, GDN_HEADS, GDN_DK, GDN_DV), jnp.float32)
    conv0 = jnp.zeros((DEPTH, B, CONV_W - 1, 3 * GDN_WIDTH), x_prompt.dtype)
    y_prompt, gla_p, gdn_p, conv_p = _trunk(x_prompt, p_prompt, gla0, gdn0, conv0, params)
    y_sample, gla_s, gdn_s, conv_s = _trunk(x_sample, p_sample, state_gla, state_gdn, state_conv, params)
    return (y_prompt, y_sample, gla_p, gdn_p, conv_p, gla_s, gdn_s, conv_s)


_drawn_inputs = setup_inputs


def setup_inputs(seed=0):
    import zlib

    import numpy as np

    out = dict(_drawn_inputs(seed))
    spreads = {}
    factors = {'gla_norm': 4.906,
     'gdn_dt_bias': 4.991,
     'gdn_norm': 5.303,
     'norm_ffn': 2.916,
     'norm_ple': 47.201,
     'b_ple_gate': 11.613,
     'norm_final': 7.807}
    for name, (base, spread) in spreads.items():
        noise = np.random.default_rng([zlib.crc32(name.encode()), seed]).standard_normal(out[name].shape)
        drawn = base * np.exp(spread * noise) if base else spread * noise
        out[name] = __import__('jax').numpy.asarray(drawn.astype(out[name].dtype))
    for name, factor in factors.items():
        out[name] = (out[name] * factor).astype(out[name].dtype)
    return out
```

```python
from contextlib import ExitStack

import concourse.bass as bass
from concourse import mybir

F32 = mybir.dt.float32
U32 = mybir.dt.uint32
ALU = mybir.AluOpType
ACT = mybir.ActivationFunctionType
AX = mybir.AxisListType.X

P = 128
EPS = 1e-6
GATE_NORM = 16.0
LOWEST = -3.0e38
TILES = 3
CONV_W = 4
GLA_CHUNK = 64
SUB = 16
TOPK = 16
G = 8
WCOLS = 256
RING = 4
BANK = 512


def hybrid_trunk(nc, x_prompt, x_sample, state_gla, state_gdn, state_conv, p_prompt, p_sample,
                 norm_mix, w_in, w_gla_up, b_gla_gate, gla_norm, conv_w, gdn_a_log, gdn_dt_bias,
                 gdn_norm, w_out, norm_ffn, w_peer_q, peer_sub_keys, peer_u, peer_v, norm_ple,
                 w_ple_gate, b_ple_gate, w_ple_proj, norm_final,
                 y_prompt, y_sample, gla_p, gdn_p, conv_p, gla_s, gdn_s, conv_s):
    DEPTH, NB, HG, DK, DV = state_gla.shape
    HD = state_gdn.shape[2]
    SEQ, D = x_prompt.shape[1:]
    TS = x_sample.shape[1]
    NSAMP = NB * TS
    NT = SEQ + NSAMP
    KD = D // P
    NEXP = peer_u.shape[1]
    HP, NK = peer_sub_keys.shape[1], peer_sub_keys.shape[3]
    PLE = p_prompt.shape[3]
    KP = PLE // P
    QD = HG * DK
    VD = HG * DV
    RANK = w_gla_up.shape[1]
    C_V1 = 2 * QD
    C_R1 = C_V1 + VD
    C_LR = C_R1 + VD
    C_QKV = C_LR + RANK
    C_Z = C_QKV + 3 * VD
    C_BA = C_Z + VD
    NQK, NC3, NH = 2 * QD // P, 3 * VD // P, 4
    ROWS = [P, P, NSAMP]
    COL = [0, P, 2 * P]
    STEPS = [HP, HP, HP // 2]
    NSTEP = sum(STEPS)
    assert SEQ == 2 * P and NSAMP == 64 and DV == P and DK == 64 and NT == 320

    blocks = [(w_in, c) for c in (0, 256, C_V1, C_V1 + 256, C_R1, C_R1 + 256)]
    blocks += [(w_in, C_QKV + WCOLS * n) for n in range(2 * 4)]
    blocks += [(w_out, WCOLS * n) for n in range(D // WCOLS)]
    blocks += [(w_peer_q, WCOLS * n) for n in range(w_peer_q.shape[2] // WCOLS)]
    blocks += [(w_ple_gate, WCOLS * n) for n in range(D // WCOLS)]
    B_OUT, B_PQ = 14, 14 + D // WCOLS
    B_PLE = B_PQ + w_peer_q.shape[2] // WCOLS

    ctx = ExitStack()
    with ctx:
        def sb(name, shape, dt=F32):
            return ctx.enter_context(nc.sbuf_tensor(name, shape, dt))

        h = sb("h", [P, TILES, D])
        xn = sb("xn", [P, TILES, D])
        aT = sb("aT", [P, KD, TILES * P])
        wring = sb("wring", [P, RING, KD, WCOLS])
        par_rows = sb("par_rows", [P, P])
        par = sb("par", [P, 76])
        PAR_MIX, PAR_FFN, PAR_PLE, PAR_CONV, PAR_GLA, PAR_GDN, PAR_BG = 0, 8, 16, 24, 72, 73, 74
        gain_row = sb("gain_row", [P, D])
        bias_row = sb("bias_row", [1, D])
        pT = sb("pT", [P, KP, TILES * P])
        ident = sb("ident", [P, P])
        twin = sb("twin", [P, P])
        ones = sb("ones", [P, P])
        zero = sb("zero", [P, P])
        incl64 = sb("incl64", [P, P])
        incl128 = sb("incl128", [P, P])
        low128 = sb("low128", [P, P])
        sub16 = sb("sub16", [P, P])
        incl8 = sb("incl8", [64, 64])
        low8 = sb("low8", [64, 64])
        same8 = sb("same8", [64, 64])
        seqmask = sb("seqmask", [64, NB])
        half_of = sb("half_of", [P, 2])
        reset = sb("reset", [P, NT])
        iota16 = sb("iota16", [P, TOPK])
        ssq = sb("ssq", [P, 4])
        rstd = sb("rstd", [P, 4])
        ad = sb("ad", [P, 2, HD])
        ba = sb("ba", [P, TILES, 2 * HD])
        beta = sb("beta", [P, TILES, HD])
        soft = sb("soft", [P, TILES, HD])
        ypos = sb("ypos", [P, TILES, HD])
        g_tok = sb("g_tok", [P, TILES, HD])
        gst = sb("gst", [P, TILES, 2 * HD])
        eb = sb("eb", [P, TILES, 2 * HD])
        kds = sb("kds", [P, TILES, HD])
        idx_u = sb("idx_u", [P, 2, TOPK], U32)
        gate = sb("gate", [P, 2, TOPK])
        hid = sb("hid", [P, 2, TOPK])
        gelu = sb("gelu", [P, 2, TOPK])
        wgt = sb("wgt", [P, 2, TOPK])
        top = sb("top", [P, 2, TOPK])
        topi = sb("topi", [P, 2, TOPK], U32)
        topf = sb("topf", [P, 2, TOPK])
        cv = sb("cv", [P, TOPK])
        ci = sb("ci", [P, TOPK], U32)
        cij = sb("cij", [P, 2, TOPK], U32)
        cijf = sb("cijf", [P, 2, TOPK])
        pick = sb("pick", [P, 2, TOPK])
        idx_f = sb("idx_f", [P, TOPK])
        ncv = sb("ncv", [P, 2])
        esum = sb("esum", [P, 2])
        gexp = sb("gexp", [P, TOPK])
        table_base = sb("table_base", [P, 1])

        ARENA = 29216
        arena = sb("arena", [P, ARENA])

        def view(off, *dims, rows=P):
            n = 1
            for d in dims:
                n *= d
            assert off + n <= ARENA, (off, dims)
            v = arena[0:rows, off:off + n]
            if len(dims) == 2:
                v = v.rearrange("p (a b) -> p a b", b=dims[1])
            elif len(dims) == 3:
                v = v.rearrange("p (a b c) -> p a b c", b=dims[1], c=dims[2])
            return v

        zs = view(0, NH, NT)
        qkvc = view(1280, NC3, NT)
        halo = view(5120, NC3, NB * (CONV_W - 1 + TS))
        raw = view(6176, NC3, NT)
        ptok = view(6176, TILES, PLE)
        k2tok = view(6176, TILES, VD)
        v2tok = view(7712, TILES, VD)
        kST = view(9248, NH, 64)
        dS = view(10016, NH, P)
        dSs = view(10528, NB, NH, P)
        vmask = view(14624, NH, NB, P, rows=64)
        l2sq = view(14624, 2 * NH * NT)
        conv_rows = view(18720, NC3 * P, rows=27)
        hist_rows = view(18720, NC3 * P, rows=24)
        lrT = view(20256, NT, rows=RANK)
        w_lrba = view(20576, KD, 24)
        tail = view(20256, NC3, 27)
        w_up = view(20768, QD, rows=RANK)
        Z = 21024
        q1k1 = view(Z, NQK, NT)
        gS = view(Z + 1280, 2, P)
        gSs = view(Z + 1536, NB * 2, P)
        gb = view(Z + 3584, 2, NT)
        q_mid = view(Z + 4224, 2, NT)
        k_mid = view(Z + 4864, 2, NT)
        k_last = view(Z + 5504, 2, NT)
        e_all = view(Z + 6144, 2, NT)
        q_all = view(Z + 6784, 2, NT)
        k_tok = view(Z + 7424, TILES, QD)
        gosq = view(Z + 4224, 2 * 640)
        attT = aT[:, 4:8, :].rearrange("p a b -> p (a b)")
        xflat = xn[:, :, :].rearrange("p a b -> p (a b)")
        v1 = xflat[:, 0:TILES * VD].rearrange("p (a b) -> p a b", b=VD)
        rs = xflat[:, TILES * VD:TILES * VD + NH * NT].rearrange("p (a b) -> p a b", b=NT)

        def slot(n, rows=P):
            flat = view(Z + 512 * n, 512) if n < 16 else xflat[:, 512 * (n - 16):512 * (n - 15)]
            return flat[0:rows, :].rearrange("p (a b) -> p a b", b=P)

        SA, SB, SC, SD, SF = [0, 7, 14], [1, 8, 15], [2, 9, 16], [3, 10, 17], [4, 11, 18]
        SO, SH, SQK = [5, 12], [6, 13], [19, 20, 21]

        def temp(i, which, rows=P):
            return view(14624 + 1024 * i + 512 * which, NH, P, rows=rows)

        def vnew(i, rows=P):
            return view(18720 + 512 * i, NH, P, rows=rows)

        k_one = view(6176, 2, 2 * NT)
        q_one = aT[:, 0:4, :].rearrange("p a b -> p (a b)")[:, 0:4 * NT].rearrange(
            "p (a b) -> p a b", a=2)
        kd = attT
        exp_b = qkvc[:, 2 * NH:3 * NH, :]
        dosq = view(Z, 2 * 640)
        oall = aT

        urow = view(0, G, D)
        vrow = view(G * D, G, D)
        keys_n = view(0, 2 * HP, P)
        qT = view(G * D, 2 * HP, TILES * P)
        scores = view(16384, NSTEP, 2, NK)
        keysT = view(21504, 2 * HP, NK)
        diag = view(23552, G, P)
        onehot = view(24576, 2, TOPK, TOPK)
        cand = view(25088, TOPK, TOPK)
        cand2 = view(25344, TOPK * TOPK)
        s_cur = view(25600, 2, NK)
        s_cut = view(25856, 2, NK)
        w_proj = view(26624, KP, D)
        sig = view(0, 2, WCOLS)

        ps = ctx.enter_context(nc.psum_tensor("ps", [P, 8, BANK], F32))

        def bank(n, rows=P, cols=BANK):
            return ps[0:rows, n, 0:cols]

        def heads(n, rows=P, cols=P):
            return ps[0:rows, n, 0:NH * P].rearrange("p (a b) -> p a b", b=P)[:, :, 0:cols]

        def sem(name):
            return ctx.enter_context(nc.semaphore(name))

        x_loaded, const_ready, layer_done, cleared = map(
            sem, ("x_loaded", "const_ready", "layer_done", "cleared"))
        fin_row, fin_sq, fin_var, fin_std, fin_step, y_ready, y_stored = map(
            sem, ("fin_row", "fin_sq", "fin_var", "fin_std", "fin_step", "y_ready",
                  "y_stored"))
        pool_made, met = map(sem, ("pool_made", "met"))
        layer_sems = []

        def lsem(name):
            layer_sems.append(sem(name))
            return layer_sems[-1]

        par_loaded = lsem("par_loaded")
        ptok_loaded = lsem("ptok_loaded")
        small_loaded = lsem("small_loaded")
        hist_loaded = lsem("hist_loaded")
        gSs_loaded = lsem("gSs_loaded")
        dSs_loaded = lsem("dSs_loaded")
        rows_loaded = lsem("rows_loaded")
        keys_loaded = lsem("keys_loaded")
        wproj_loaded = lsem("wproj_loaded")
        w_loaded = [lsem(f"w_loaded{r}") for r in range(RING)]
        block_used = lsem("block_used")
        first_T = lsem("first_T")
        par_ready = lsem("par_ready")
        pT_ready = lsem("pT_ready")
        hist_ready = lsem("hist_ready")
        sq_done = lsem("sq_done")
        var_ready = lsem("var_ready")
        std_ready = lsem("std_ready")
        xn_ready = lsem("xn_ready")
        xT_done = lsem("xT_done")
        aT_ready = lsem("aT_ready")
        unit_mm = lsem("unit_mm")
        unit_out = lsem("unit_out")
        y_in = lsem("y_in")
        soft_ready = lsem("soft_ready")
        g_ready = lsem("g_ready")
        gate_mm = lsem("gate_mm")
        gx_ready = lsem("gx_ready")
        gl_args = lsem("gl_args")
        gl_exps = lsem("gl_exps")
        gl_ops = lsem("gl_ops")
        one_ready = lsem("one_ready")
        kd_T = lsem("kd_T")
        k_tok_ready = lsem("k_tok_ready")
        att_mm = lsem("att_mm")
        att_ready = lsem("att_ready")
        gU_mm = lsem("gU_mm")
        gS_ready = lsem("gS_ready")
        go_mm = lsem("go_mm")
        gvm_ready = lsem("gvm_ready")
        gs_decayed = lsem("gs_decayed")
        gs_mm = lsem("gs_mm")
        gs_add = lsem("gs_add")
        on_sq = lsem("on_sq")
        on_sum = lsem("on_sum")
        on_var = lsem("on_var")
        on_std = lsem("on_std")
        o_ready = lsem("o_ready")
        conv_done = lsem("conv_done")
        qkv_act = lsem("qkv_act")
        tail_ready = lsem("tail_ready")
        conv_rows_ready = lsem("conv_rows_ready")
        l2_sq = lsem("l2_sq")
        l2_sum = lsem("l2_sum")
        l2_var = lsem("l2_var")
        l2_std = lsem("l2_std")
        qk_ready = lsem("qk_ready")
        k2_T = lsem("k2_T")
        k2tok_ready = lsem("k2tok_ready")
        v2_T = lsem("v2_T")
        v2tok_ready = lsem("v2tok_ready")
        gst_mm = lsem("gst_mm")
        gst_ready = lsem("gst_ready")
        gst_exp = lsem("gst_exp")
        kd_ready = lsem("kd_ready")
        bB_mm = lsem("bB_mm")
        G_mm = lsem("G_mm")
        dargs = lsem("dargs")
        dexp = lsem("dexp")
        P1_ready = lsem("P1_ready")
        P1T_mm = lsem("P1T_mm")
        P1T_out = lsem("P1T_out")
        F0_ready = lsem("F0_ready")
        qk_mm = lsem("qk_mm")
        qkT_ready = lsem("qkT_ready")
        qd_ready = lsem("qd_ready")
        solve_mm = lsem("solve_mm")
        solve_act = lsem("solve_act")
        solve_dve = lsem("solve_dve")
        kS_mm = lsem("kS_mm")
        kST_mm = lsem("kST_mm")
        kST_ready = lsem("kST_ready")
        r_ready = lsem("r_ready")
        y_mm = lsem("y_mm")
        y_out = lsem("y_out")
        vn_mm = lsem("vn_mm")
        vn_ready = lsem("vn_ready")
        do_mm = lsem("do_mm")
        dU_mm = lsem("dU_mm")
        dS_ready = lsem("dS_ready")
        dvm_ready = lsem("dvm_ready")
        ds_decayed = lsem("ds_decayed")
        ds_mm = lsem("ds_mm")
        ds_add = lsem("ds_add")
        stored = [lsem(f"stored_{n}") for n in ("gla_p", "gla_s", "conv_p", "conv_s", "gdn_p", "gdn_s")]
        mix_mm = lsem("mix_mm")
        mix_add = lsem("mix_add")
        q_mm = lsem("q_mm")
        q_out = lsem("q_out")
        key_T = lsem("key_T")
        key_out = lsem("key_out")
        score_mm = lsem("score_mm")
        score_out = lsem("score_out")
        cv_ready = lsem("cv_ready")
        gate_exp = lsem("gate_exp")
        idx_ready = lsem("idx_ready")
        u_loaded = [lsem(f"u_loaded{r}") for r in range(G)]
        v_loaded = [lsem(f"v_loaded{r}") for r in range(G)]
        u_free = lsem("u_free")
        v_free = lsem("v_free")
        gathers = lsem("gathers")
        gelu_ready = lsem("gelu_ready")
        wgt_ready = lsem("wgt_ready")
        diag_ready = lsem("diag_ready")
        h_added = lsem("h_added")
        ple_mm = lsem("ple_mm")
        ple_sig = lsem("ple_sig")
        ple_done = lsem("ple_done")
        act_step = lsem("act_step")
        dve_step = lsem("dve_step")
        pick_step = sem("pick_step")
        first, last = layer_sems[0].num, layer_sems[-1].num
        assert last - first == len(layer_sems) - 1

        class Steps:

            def __init__(self, eng, own):
                self.eng, self.own, self.n = eng, own, 0

            def after(self, ins):
                self.n += 1
                ins.then_inc(self.own, 1)

            def settle(self):
                self.eng.wait_ge(self.own, self.n)

        def meet(eng, layer):
            eng.drain().then_inc(layer_done, 1)
            eng.wait_ge(cleared, layer + 1)

        def row(t, layer):
            return t[bass.ds(layer, 1), :]

        def of(t, layer):
            s = t[(bass.ds(layer, 1),) + (slice(None),) * (len(t.shape) - 1)]
            names = " ".join("abcdef"[:len(t.shape) - 1])
            first_, rest = names[0], names[2:]
            return s.rearrange(f"o {names} -> (o {first_}) {rest}")

        block = ctx.enter_context(nc.Block())
        xp = x_prompt.rearrange("o (i p) d -> p (o i) d", p=P)
        xs = x_sample.rearrange("b t d -> (b t) d")

        @block.sync
        def _(sp):
            sp.dma_start(h[:, 0:2, :], xp).then_inc(x_loaded, 16)
            sp.dma_start(h[0:64, 2, :], xs).then_inc(x_loaded, 16)
            sp.dma_start(h[64:P, 2, :], xs).then_inc(x_loaded, 16)
            with sp.Fori(0, DEPTH) as layer:
                for t, r0, n in ((norm_mix, PAR_MIX, KD), (norm_ffn, PAR_FFN, KD),
                                 (norm_ple, PAR_PLE, KD), (gla_norm, PAR_GLA, 1),
                                 (gdn_norm, PAR_GDN, 1), (b_gla_gate, PAR_BG, 2)):
                    sp.dma_start(par_rows[r0:r0 + n, :],
                                 row(t, layer).rearrange("o (k p) -> (o k) p", p=P)
                                 ).then_inc(par_loaded, 16)
                sp.dma_start(par_rows[PAR_CONV:PAR_CONV + CONV_W * NC3, :],
                             conv_w[bass.ds(layer, 1), :, :].rearrange("o j (k p) -> (o j k) p", p=P)
                             ).then_inc(par_loaded, 16)
                pp = p_prompt[bass.ds(layer, 1), 0, :, :].rearrange("o (i p) d -> p (o i) d", p=P)
                pz = p_sample[bass.ds(layer, 1), :, :, :].rearrange("o b t d -> (o b t) d")
                sp.dma_start(ptok[:, 0:2, :], pp).then_inc(ptok_loaded, 16)
                sp.dma_start(ptok[0:64, 2, :], pz).then_inc(ptok_loaded, 16)
                sp.dma_start(ptok[64:P, 2, :], pz).then_inc(ptok_loaded, 16)
                w_l = w_in[bass.ds(layer, 1), :, :]
                sp.dma_start(w_lrba[:, :, 0:RANK],
                             w_l[:, :, C_LR:C_LR + RANK].rearrange("o (k p) n -> p (o k) n", p=P)
                             ).then_inc(small_loaded, 16)
                sp.dma_start(w_lrba[:, :, RANK:24],
                             w_l[:, :, C_BA:C_BA + 2 * HD].rearrange("o (k p) n -> p (o k) n", p=P)
                             ).then_inc(small_loaded, 16)
                sp.dma_start(w_up[:, :], of(w_gla_up, layer)).then_inc(small_loaded, 16)
                sp.dma_start(ad[:, 0, :], row(gdn_a_log, layer).to_broadcast([P, HD])
                             ).then_inc(small_loaded, 16)
                sp.dma_start(ad[:, 1, :], row(gdn_dt_bias, layer).to_broadcast([P, HD])
                             ).then_inc(small_loaded, 16)
                sp.dma_start(hist_rows[:, :], state_conv[bass.ds(layer, 1), :, :, :].rearrange(
                    "o b j c -> (o b j) c")).then_inc(hist_loaded, 16)

                def load_block(n):
                    t, c = blocks[n]
                    if n >= RING:
                        sp.wait_ge(block_used, n - RING + 1)
                    sp.dma_start(wring[:, n % RING, :, :],
                                 t[bass.ds(layer, 1), :, c:c + WCOLS].rearrange(
                                     "o (k p) n -> p (o k) n", p=P)).then_inc(w_loaded[n % RING], 16)

                for n in range(RING):
                    load_block(n)
                sp.dma_start(gain_row[:, :], row(norm_ffn, layer).to_broadcast([P, D])
                             ).then_inc(rows_loaded, 16)
                sp.dma_start(bias_row[:, :], row(b_ple_gate, layer)).then_inc(rows_loaded, 16)
                for n in range(RING, B_PQ + RING):
                    load_block(n)
                sp.wait_ge(mix_add, 12)
                for n in range(B_PQ + RING, len(blocks)):
                    load_block(n)
                sp.dma_start(w_proj[:, :, :], w_ple_proj[bass.ds(layer, 1), :, :].rearrange(
                    "o (k p) n -> p (o k) n", p=P)).then_inc(wproj_loaded, 16)
                sp.drain().then_inc(layer_done, 1)
                sp.wait_ge(layer_done, (layer + 1) * 5)
                sp.sem_inc(met, 1)
                sp.sem_clear(range(first, last + 1))
                sp.drain().then_inc(cleared, 1)
            sp.dma_start(gain_row[:, :], norm_final.rearrange("(o d) -> o d", o=1).to_broadcast([P, D])
                         ).then_inc(fin_row, 16)
            sp.wait_ge(y_ready, 3)
            sp.dma_start(y_prompt.rearrange("o (i p) d -> p (o i) d", p=P), xn[:, 0:2, :]
                         ).then_inc(y_stored, 16)
            sp.dma_start(y_sample.rearrange("b t d -> (b t) d"), xn[0:64, 2, :]
                         ).then_inc(y_stored, 16)
            sp.wait_ge(y_stored, 32)

        @block.gpsimd
        def _(pool):
            made = Steps(pool, pool_made)
            for t, value in ((ident, 0.0), (twin, 0.0), (ones, 1.0), (zero, 0.0), (incl64, 1.0),
                             (incl128, 1.0), (low128, 1.0), (sub16, 1.0), (incl8, 1.0), (low8, 1.0),
                             (same8, 1.0), (seqmask, 1.0), (half_of, 1.0), (reset, 1.0), (ba, 0.0), (gst, 0.0),
                             (table_base, 0.0), (hid, 0.0)):
                made.after(pool.memset(t[:], value))
            made.after(pool.iota(iota16[:, :], pattern=[[1, TOPK]], base=0, channel_multiplier=0,
                                 allow_small_or_imprecise_dtypes=True))
            made.settle()

            def select(t, pattern, base, mult, op=ALU.is_ge, fill=0.0):
                made.after(pool.affine_select(out=t, in_=t, compare_op=op, fill=fill, base=base,
                                              pattern=pattern, channel_multiplier=mult))
                made.settle()

            def same_block(t, nb, size):
                v = t[:, :].rearrange("p (b j) -> p b j", j=size)
                select(v, [[-size, nb], [0, size]], 0, 1)
                select(v, [[size, nb], [0, size]], size - 1, -1)

            select(ident[:, :], [[-1, P]], 0, 1, ALU.not_equal, 1.0)
            for off in (0, 64, -64):
                select(twin[:, :], [[-1, P]], off, 1, ALU.not_equal, 1.0)
            same_block(incl64, 2, GLA_CHUNK)
            same_block(sub16, P // SUB, SUB)
            for t in (incl8, low8, same8):
                same_block(t, NB, TS)
            for t, n in ((incl64, P), (incl128, P), (incl8, 64)):
                select(t[:, :], [[1, n]], 0, -1)
            for t, n in ((low128, P), (low8, 64)):
                select(t[:, :], [[-1, n]], -1, 1)
            select(seqmask[:, :], [[-TS, NB]], 0, 1)
            select(half_of[:, 0:1], [[0, 1]], 63, -1)
            select(half_of[:, 1:2], [[0, 1]], -64, 1)
            select(seqmask[:, :], [[TS, NB]], TS - 1, -1)
            for v, n in ((reset[:, 0:SEQ].rearrange("p (c t) -> p c t", t=GLA_CHUNK), GLA_CHUNK),
                         (reset[:, SEQ:NT].rearrange("p (c t) -> p c t", t=TS), TS)):
                select(v, [[0, v.shape[1]], [1, n]], -1, 0)
            pool.sem_inc(const_ready, 1)

            with pool.Fori(0, DEPTH) as layer:
                pool.dma_start(gSs[:, :, :], state_gla[bass.ds(layer, 1), :, :, :, :].rearrange(
                    "o b (r s) k v -> (s k) (o b r) v", s=2)).then_inc(gSs_loaded, 16)
                pool.dma_start(dSs.rearrange("p b g v -> p (b g) v"),
                             state_gdn[bass.ds(layer, 1), :, :, :, :].rearrange(
                                 "o b g k v -> k (o b g) v")).then_inc(dSs_loaded, 16)
                pool.wait_ge(unit_out, 12)
                for hd in range(NH):
                    ins = pool.tensor_tensor(
                        vmask[:, hd, :, :],
                        v1[0:64, 2, hd * P:(hd + 1) * P].unsqueeze(1).to_broadcast([64, NB, P]),
                        seqmask[:, :].unsqueeze(2).to_broadcast([64, NB, P]), ALU.mult)
                ins.then_inc(gvm_ready, 1)
                pool.wait_ge(go_mm, 3)
                for r in range(2):
                    d = e_all[:, r, SEQ:NT].rearrange("p (b t) -> p b t", t=TS)[:, :, TS - 1:TS]
                    s_ = gSs[:, :, :].rearrange("p (b r) v -> p b r v", r=2)[:, :, r, :]
                    ins = pool.tensor_tensor(s_, s_, d.to_broadcast([P, NB, P]), ALU.mult)
                ins.then_inc(gs_decayed, 1)
                pool.wait_ge(gS_ready, 4)
                pool.dma_start(gla_p[bass.ds(layer, 1), 0, :, :, :].rearrange(
                    "o (r s) k v -> (s k) (o r) v", s=2), gS[:, :, :]).then_inc(stored[0], 16)
                pool.wait_ge(gs_add, 8)
                pool.dma_start(gla_s[bass.ds(layer, 1), :, :, :, :].rearrange(
                    "o b (r s) k v -> (s k) (o b r) v", s=2), gSs[:, :, :]
                ).then_inc(stored[1], 16)
                pool.wait_ge(conv_rows_ready, 1)
                pool.dma_start(conv_p[bass.ds(layer, 1), 0, :, :].rearrange("o j c -> (o j) c"),
                               conv_rows[0:3, :]).then_inc(stored[2], 16)
                pool.dma_start(conv_s[bass.ds(layer, 1), :, :, :].rearrange("o b j c -> (o b j) c"),
                               conv_rows[3:27, :]).then_inc(stored[3], 16)
                pool.wait_ge(k2tok_ready, 3)
                pool.wait_ge(gst_exp, 1)
                for i in range(TILES):
                    R = ROWS[i]
                    ins = pool.tensor_tensor(
                        kd[0:R, i * VD:(i + 1) * VD].rearrange("p (a b) -> p a b", b=P),
                        k2tok[0:R, i, :].rearrange("p (a b) -> p a b", b=P),
                        kds[0:R, i, :].unsqueeze(2).to_broadcast([R, NH, P]), ALU.mult)
                ins.then_inc(kd_ready, 1)
                pool.wait_ge(dexp, 3)
                pool.wait_ge(qk_mm, 3)
                pool.tensor_tensor(qkvc[:, 0:NH, :], qkvc[:, 0:NH, :], exp_b[:, :, :],
                                   ALU.mult).then_inc(qd_ready, 1)
                pool.wait_ge(vn_ready, 3)
                for hd in range(NH):
                    ins = pool.tensor_tensor(
                        vmask[:, hd, :, :],
                        vnew(2, 64)[:, hd, :].unsqueeze(1).to_broadcast([64, NB, P]),
                        seqmask[:, :].unsqueeze(2).to_broadcast([64, NB, P]), ALU.mult)
                ins.then_inc(dvm_ready, 1)
                pool.wait_ge(do_mm, 3)
                for hd in range(NH):
                    d = exp_b[:, hd, SEQ:NT].rearrange("p (b t) -> p b t", t=TS)[:, :, TS - 1:TS]
                    ins = pool.tensor_tensor(dSs[:, :, hd, :], dSs[:, :, hd, :],
                                             d.to_broadcast([P, NB, P]), ALU.mult)
                ins.then_inc(ds_decayed, 1)
                pool.wait_ge(dS_ready, 2)
                pool.dma_start(gdn_p[bass.ds(layer, 1), 0, :, :, :].rearrange(
                    "o g k v -> k (o g) v"), dS[:, :, :]).then_inc(stored[4], 16)
                pool.wait_ge(ds_add, 8)
                pool.dma_start(gdn_s[bass.ds(layer, 1), :, :, :, :].rearrange(
                    "o b g k v -> k (o b g) v"), dSs.rearrange("p b g v -> p (b g) v")
                ).then_inc(stored[5], 16)
                for done in stored:
                    pool.wait_ge(done, 16)
                pool.wait_ge(mix_add, 12)
                pool.dma_start(keys_n[:, :, :], peer_sub_keys[bass.ds(layer, 1), :, :, :, :].rearrange(
                    "o g c n d -> n (o g c) d")).then_inc(keys_loaded, 16)
                pool.wait_ge(score_out, 12)
                u_l = peer_u.rearrange("l e d -> (l e) d")
                v_l = peer_v.rearrange("l e d -> (l e) d")

                def gather_pair(pair):
                    for par_ in range(2):
                        step = pair * 2 + par_
                        pool.wait_ge(idx_ready, step + 1)
                        for half in range(2):
                            done = step * TOPK + half * G
                            for r in range(G):
                                at = idx_u[:, par_, half * G + r:half * G + r + 1]
                                pool.wait_ge(u_free, done + r + 1)
                                pool.sem_inc(gathers, 1)
                                pool.indirect_dma_start(
                                    urow[:, r, :], None, u_l,
                                    bass.IndirectOffsetOnAxis(ap=at, axis=0)).then_inc(u_loaded[r], 16)
                            for r in range(G):
                                at = idx_u[:, par_, half * G + r:half * G + r + 1]
                                pool.wait_ge(v_free, done + r + 1)
                                pool.sem_inc(gathers, 1)
                                pool.indirect_dma_start(
                                    vrow[:, r, :], None, v_l,
                                    bass.IndirectOffsetOnAxis(ap=at, axis=0)).then_inc(v_loaded[r], 16)

                with pool.Fori(0, NSTEP // 2) as pair:
                    gather_pair(pair)
                pool.wait_ge(u_free, G + NSTEP * TOPK)
                pool.wait_ge(v_free, G + NSTEP * TOPK)
                pool.dma_reset(range(first, last + 1))
                meet(pool, layer)

        units = [("lr", 0, None), ("ba", 0, None)]
        units += [("q1k1", f, f // 2) for f in range(NQK)]
        units += [("v1", (m, i), 2 + m) for m in range(2) for i in range(TILES)]
        units += [("r1", f, 4 + f // 2) for f in range(NH)]
        units += [("qkv", f, 6 + f // 2) for f in range(NC3)]
        units += [("z", f, 12 + f // 2) for f in range(NH)]
        U_QKV = 16

        solve = [(SC, SB, SA, "act"), (SD, SA, SB, "dve"), (SF, SC, SF, "+"),
                 (SA, SD, SC, "act"), (SB, SC, SD, "dve"), (SF, SA, SF, "+"),
                 (SC, SB, SA, "act"), (SF, SC, SF, "+"),
                 (SA, SF, SO, "act"), (SB, SO, SF, "dve"), (SC, SB, SA, "act"),
                 (SD, SA, SB, "dve"), (SH, SC, SH, "+"), (SA, SD, SC, "act"), (SH, SA, SH, "+")]
        INNER, N_T = 6, 9

        def solve_tiles(k):
            return (0, 1, 2) if k < INNER else (0, 1)

        def evacuations(upto, who):
            return sum(len(solve_tiles(k)) for k in range(upto) if (solve[k][3] == "act") == (who == "act"))

        @block.scalar
        def _(act):
            def norm(use, own):
                for i in range(TILES):
                    act.activation(xn[:, i, :], h[:, i, :], ACT.Square,
                                   accum_out=ssq[:, i:i + 1]).then_inc(sq_done, 1)
                act.wait_ge(var_ready, use + 1)
                act.activation(rstd[:, 0:3], ssq[:, 0:3], ACT.Sqrt).then_inc(std_ready, 1)
                for k in range(KD):
                    act.wait_ge(xT_done, KD * use + k + 1)
                    src = ps[:, k % 2, 0:TILES * P]
                    if use == 1:
                        ins = act.activation(aT[:, k, :], src, ACT.Copy)
                    else:
                        g0 = (PAR_MIX if use == 0 else PAR_PLE) + k
                        ins = act.activation(aT[:, k, :], src, ACT.Copy, scale=par[:, g0:g0 + 1])
                    ins.then_inc(aT_ready, 1)

            def out_norm(which, own):
                made = go_mm if which == 0 else do_mm
                sq = gosq if which == 0 else dosq
                for i in range(TILES):
                    R = ROWS[i]
                    act.wait_ge(made, i + 1)
                    if which == 0:
                        act.wait_ge(att_ready, 3)
                    act.activation(sq[:, 512 * i:512 * i + NH * R].rearrange("p (a b) -> p a b", b=R),
                                   heads(3 + i, P, R), ACT.Square).then_inc(on_sq, 1)
                for i in range(TILES):
                    R = ROWS[i]
                    act.wait_ge(on_var, TILES * which + i + 1)
                    v = sq[:, 512 * i:512 * i + NH * R]
                    act.activation(v, v, ACT.Sqrt).then_inc(on_std, 1)

            act.wait_ge(const_ready, 1)
            act.wait_ge(x_loaded, 48)
            with act.Fori(0, DEPTH) as layer:
                own = Steps(act, act_step)
                act.wait_ge(first_T, 2)
                act.activation(pT[:, 0, :], ps[:, 5, 0:TILES * P], ACT.Copy)
                act.activation(pT[:, 1, :], ps[:, 6, 0:TILES * P], ACT.Copy).then_inc(pT_ready, 1)
                act.wait_ge(par_ready, 1)
                norm(0, own)

                def conv_silu(f):
                    act.wait_ge(conv_done, f + 1)
                    act.activation(qkvc[:, f, :], qkvc[:, f, :], ACT.Silu).then_inc(qkv_act, 1)

                for n, (name, f, blk) in enumerate(units):
                    b = 2 + n % 4
                    act.wait_ge(unit_mm, n + 1)
                    if name == "lr":
                        ins = act.activation(lrT[:, :], ps[0:RANK, b, 0:NT], ACT.Copy)
                    elif name == "ba":
                        act.activation(ba[:, 0:2, :], ps[:, b, 0:16].rearrange(
                            "p (i n) -> p i n", n=8), ACT.Copy)
                        ins = act.activation(ba[0:64, 2, :], ps[0:64, b, 16:24], ACT.Copy)
                    elif name == "q1k1":
                        ins = act.activation(q1k1[:, f, :], ps[:, b, 0:NT], ACT.Copy)
                    elif name == "v1":
                        m, i = f
                        R = ROWS[i]
                        ins = act.activation(v1[0:R, i, WCOLS * m:WCOLS * (m + 1)],
                                             ps[0:R, b, 0:WCOLS], ACT.Copy)
                    elif name == "r1":
                        ins = act.activation(rs[:, f, :], ps[:, b, 0:NT], ACT.Silu)
                    elif name == "z":
                        ins = act.activation(zs[:, f, :], ps[:, b, 0:NT], ACT.Silu)
                    else:
                        if f == 0:
                            act.wait_ge(hist_ready, 1)
                        act.activation(raw[:, f, 0:SEQ], ps[:, b, 0:SEQ], ACT.Copy)
                        ins = act.activation(
                            halo[:, f, :].rearrange("p (b t) -> p b t", b=NB)[:, :, CONV_W - 1:],
                            ps[:, b, SEQ:NT].rearrange("p (b t) -> p b t", b=NB), ACT.Copy)
                    ins.then_inc(unit_out, 1)
                    if name == "qkv" and f >= 2:
                        conv_silu(f - 2)
                    if n == 5:
                        act.wait_ge(gate_mm, 1)
                        for r in range(2):
                            own.after(act.activation(gb[:, r, :], ps[:, 6 + r, 0:NT], ACT.Identity,
                                                     bias=par[:, PAR_BG + r:PAR_BG + r + 1]))
                        act.wait_ge(y_in, 1)
                        own.after(act.activation(soft[:, :, :], ypos[:, :, :], ACT.Abs))
                        own.settle()
                        own.after(act.activation(q_mid[:, :, :], gb[:, :, :], ACT.Abs))
                        own.settle()
                        own.after(act.activation(soft[:, :, :], soft[:, :, :], ACT.Exp, scale=-1.0))
                        own.after(act.activation(q_mid[:, :, :], q_mid[:, :, :], ACT.Exp, scale=-1.0))
                        own.after(act.activation(ad[:, 0, :], ad[:, 0, :], ACT.Exp))
                        own.settle()
                        act.activation(soft[:, :, :], soft[:, :, :], ACT.Ln, bias=ones[:, 0:1])
                        act.activation(q_mid[:, :, :], q_mid[:, :, :], ACT.Ln,
                                       bias=ones[:, 0:1]).then_inc(gx_ready, 1)
                        act.activation(beta[:, :, :], ba[:, :, 0:HD], ACT.Sigmoid
                                       ).then_inc(soft_ready, 1)
                    if n == 11:
                        act.wait_ge(gl_args, 1)
                        s = 1.0 / GATE_NORM
                        own.after(act.activation(k_mid[:, :, :], q_mid[:, :, :], ACT.Exp, scale=-s))
                        own.settle()
                        act.activation(q_mid[:, :, :], q_mid[:, :, :], ACT.Exp, scale=s)
                        act.activation(k_last[:, :, :], k_last[:, :, :], ACT.Exp, scale=-s)
                        act.activation(e_all[:, :, :], gb[:, :, :], ACT.Exp, scale=s
                                       ).then_inc(gl_exps, 1)
                conv_silu(NC3 - 2)
                conv_silu(NC3 - 1)

                act.wait_ge(kd_T, 1)
                act.activation(k_tok[:, 0:2, :].rearrange("p a b -> p (a b)"), bank(6), ACT.Copy)
                act.activation(k_tok[0:64, 2, :], ps[0:64, 7, 0:QD], ACT.Copy
                               ).then_inc(k_tok_ready, 1)
                out_norm(0, own)
                act.wait_ge(first_T, 4)
                for b in range(3):
                    ins = act.activation(conv_rows[:, 512 * b:512 * (b + 1)], bank(b, 27), ACT.Copy)
                ins.then_inc(conv_rows_ready, 1)
                act.wait_ge(gs_mm, 8)
                act.wait_ge(gvm_ready, 1)
                act.wait_ge(qkv_act, NC3)
                act.activation(l2sq[:, :], qkvc[:, 0:2 * NH, :].rearrange("p a b -> p (a b)"),
                               ACT.Square).then_inc(l2_sq, 1)
                act.wait_ge(l2_var, 1)
                act.activation(l2sq[:, :], l2sq[:, :], ACT.Sqrt).then_inc(l2_std, 1)
                for i in range(TILES):
                    act.wait_ge(v2_T, i + 1)
                    act.activation(v2tok[0:ROWS[i], i, :], bank(3 + i, ROWS[i]), ACT.Copy
                                   ).then_inc(v2tok_ready, 1)
                for i in range(TILES):
                    act.wait_ge(k2_T, i + 1)
                    act.activation(k2tok[0:ROWS[i], i, :], bank(i, ROWS[i]), ACT.Copy
                                   ).then_inc(k2tok_ready, 1)
                act.wait_ge(gst_ready, 1)
                act.activation(eb[:, :, :], gst[:, :, :], ACT.Exp)
                act.activation(kds[:, :, :], kds[:, :, :], ACT.Exp).then_inc(gst_exp, 1)
                for i in range(TILES):
                    R = ROWS[i]
                    act.wait_ge(dargs, i + 1)
                    act.activation(temp(i, 0, R)[:, :, 0:R], temp(i, 0, R)[:, :, 0:R], ACT.Exp,
                                   scale=-1.0)
                    act.activation(temp(i, 1, R)[:, :, 0:R], temp(i, 1, R)[:, :, 0:R], ACT.Exp)
                    act.wait_ge(v2_T, 3)
                    act.activation(exp_b[:, :, COL[i]:COL[i] + R], heads(i, P, R), ACT.Exp
                                   ).then_inc(dexp, 1)
                for i in range(TILES):
                    R = ROWS[i]
                    act.wait_ge(P1T_mm, i + 1)
                    act.activation(slot(SB[i], R)[:, :, 0:R], heads(3 + i, R, R), ACT.Copy
                                   ).then_inc(P1T_out, 1)
                n = 0
                for k, (to, _, _, who) in enumerate(solve):
                    for i in solve_tiles(k):
                        n += 1
                        if who == "act":
                            R = ROWS[i]
                            act.wait_ge(solve_mm, n)
                            act.activation(slot(to[i], R)[:, :, 0:R], heads(i + 3 * (k % 2), R, R),
                                           ACT.Copy).then_inc(solve_act, 1)
                for i in range(TILES):
                    R = ROWS[i]
                    if i < 2:
                        act.wait_ge(y_mm, i + 1)
                        act.activation(temp(i, 0), heads(1), ACT.Copy).then_inc(y_out, 1)
                    else:
                        act.wait_ge(kST_mm, 1)
                        act.activation(kST[:, :, :], ps[:, 7, 0:256].rearrange(
                            "p (a b) -> p a b", b=64), ACT.Copy).then_inc(kST_ready, 1)
                    act.wait_ge(vn_mm, i + 1)
                    if i == 0:
                        for done in stored[2:4]:
                            act.wait_ge(done, 16)
                    act.activation(vnew(i, R), heads(2, R), ACT.Copy).then_inc(vn_ready, 1)
                out_norm(1, own)

                act.wait_ge(mix_add, 12)
                norm(1, own)
                for n in range(2 * HP):
                    act.wait_ge(q_mm, n + 1)
                    src = ps[:, 2 + n % 4, :]
                    act.activation(qT[:, n, 0:NT], src[:, 0:NT], ACT.Copy)
                    act.activation(qT[:, n, NT:], src[:, SEQ:NT], ACT.Copy).then_inc(q_out, 1)
                for n in range(12):
                    i, m = n // 4, n % 4
                    act.wait_ge(score_mm, n + 1)
                    r0, r1, s0 = 0, P, HP * i + 2 * m
                    if i == 2:
                        r0, r1, s0 = (0, 64, 16 + 2 * m) if m < 2 else (64, P, 16 + 2 * (m - 2))
                    act.activation(scores[r0:r1, s0:s0 + 2, :, :].rearrange("p a b c -> p (a b c)"),
                                   ps[r0:r1, (6 + n % 4) % 8, :], ACT.Copy).then_inc(score_out, 1)

                def softmax(step):
                    act.wait_ge(cv_ready, step + 1)
                    act.activation(gexp[:, :], cv[:, :], ACT.Exp, bias=ncv[:, 0:1],
                                   accum_out=esum[:, 0:1]).then_inc(gate_exp, 1)

                def weights(step, par_, half, unit):
                    c = slice(half * G, half * G + G)
                    done = step * TOPK + half * G
                    act.wait_ge(u_free, done + 2 * G)
                    act.activation(gelu[:, par_, c], hid[:, par_, c], ACT.Gelu
                                   ).then_inc(gelu_ready, 1)
                    act.wait_ge(wgt_ready, step * 2 + half + 1)
                    for r in range(G):
                        act.wait_ge(v_free, done + r + 1)
                        k = half * G + r
                        act.activation(diag[:, r, :], unit[:, :], ACT.Copy,
                                       scale=wgt[:, par_, k:k + 1]).then_inc(diag_ready, 1)

                softmax(0)

                def pair_of(pair, unit, is_last=False):
                    for par_ in range(2):
                        step = pair * 2 + par_
                        weights(step, par_, 0, unit)
                        if not (is_last and par_):
                            softmax(step + 1)
                        weights(step, par_, 1, unit)

                with act.Fori(0, HP) as pair:
                    pair_of(pair, ident)
                pair_of(HP, twin)
                pair_of(HP + 1, twin, is_last=True)
                act.wait_ge(h_added, 3)
                norm(2, own)
                for n in range(12):
                    act.wait_ge(ple_mm, n + 1)
                    if n >= 2:
                        act.wait_ge(ple_done, n - 1)
                    act.activation(sig[:, n % 2, :], ps[:, 4 + n % 4, 0:WCOLS], ACT.Sigmoid
                                   ).then_inc(ple_sig, 1)
                meet(act, layer)
            for i in range(TILES):
                act.activation(xn[:, i, :], h[:, i, :], ACT.Square,
                               accum_out=ssq[:, i:i + 1]).then_inc(fin_sq, 1)
            act.wait_ge(fin_var, 1)
            act.activation(rstd[:, 0:3], ssq[:, 0:3], ACT.Sqrt).then_inc(fin_std, 1)

        @block.vector
        def _(dve):
            def norm(use, own):
                dve.wait_ge(sq_done, TILES * (use + 1))
                dve.tensor_scalar(ssq[:, 0:3], ssq[:, 0:3], 1.0 / D, EPS, ALU.mult, ALU.add
                                  ).then_inc(var_ready, 1)
                dve.wait_ge(std_ready, use + 1)
                own.after(dve.reciprocal(rstd[:, 0:3], rstd[:, 0:3]))
                own.settle()
                if use == 1:
                    dve.wait_ge(rows_loaded, 32)
                for i in range(TILES):
                    if use == 1:
                        ins = dve.scalar_tensor_tensor(xn[:, i, :], h[:, i, :], rstd[:, i:i + 1],
                                                       gain_row[:, :], ALU.mult, ALU.mult)
                    else:
                        ins = dve.tensor_scalar(xn[:, i, :], h[:, i, :], rstd[:, i:i + 1], None,
                                                ALU.mult)
                    ins.then_inc(xn_ready, 1)

            def over_heads(t, R):
                return t[0:R, 0:R].unsqueeze(1).to_broadcast([R, NH, R])

            def per_head(t, R, n=P):
                return t.unsqueeze(2).to_broadcast([R, NH, n])

            def out_norm(which, own):
                sq = gosq if which == 0 else dosq
                gain = par[:, PAR_GLA + which:PAR_GLA + which + 1]
                for i in range(TILES):
                    R = ROWS[i]
                    v = sq[:, 512 * i:512 * i + NH * R]
                    dve.wait_ge(on_sum, TILES * which + i + 1)
                    dve.tensor_scalar(v, ps[:, 6 + i % 2, 0:NH * R], 1.0 / P, EPS, ALU.mult,
                                      ALU.add).then_inc(on_var, 1)
                for i in range(TILES):
                    R = ROWS[i]
                    v = sq[:, 512 * i:512 * i + NH * R]
                    v3 = v.rearrange("p (a b) -> p a b", b=R)
                    dve.wait_ge(on_std, TILES * which + i + 1)
                    own.after(dve.reciprocal(v, v))
                    own.settle()
                    own.after(dve.tensor_tensor(v3, v3, heads(3 + i, P, R), ALU.mult))
                    own.settle()
                    silu = (rs if which == 0 else zs)[:, :, COL[i]:COL[i] + R]
                    o4 = oall[:, 4 * which:4 * which + 4, :]
                    ins = dve.scalar_tensor_tensor(o4[:, :, COL[i]:COL[i] + R], v3, gain, silu,
                                                   ALU.mult, ALU.mult)
                    if i == 2:
                        ins = dve.scalar_tensor_tensor(o4[:, :, NT:NT + R], v3, gain, silu,
                                                       ALU.mult, ALU.mult)
                    ins.then_inc(o_ready, 1)

            def pick_experts(step, par_):
                own = Steps(dve, pick_step)
                own.after(dve.tensor_copy(s_cur[:, :, :], scores[:, bass.ds(step, 1), :, :]
                                          .rearrange("p o c n -> p (o c) n")))
                own.settle()
                for c in range(2):
                    own.after(dve.max(top[:, c, 0:8], s_cur[:, c, :]))
                own.settle()
                for c in range(2):
                    own.after(dve.match_replace(s_cut[:, c, :], top[:, c, 0:8], s_cur[:, c, :],
                                                LOWEST))
                    own.after(dve.max_index(topi[:, c, 0:8], top[:, c, 0:8], s_cur[:, c, :]))
                own.settle()
                for c in range(2):
                    own.after(dve.max(top[:, c, 8:16], s_cut[:, c, :]))
                own.settle()
                own.after(dve.tensor_tensor(
                    cand[:, :, :], top[:, 0, :].unsqueeze(2).to_broadcast([P, TOPK, TOPK]),
                    top[:, 1, :].unsqueeze(1).to_broadcast([P, TOPK, TOPK]), ALU.add))
                for c in range(2):
                    own.after(dve.max_index(topi[:, c, 8:16], top[:, c, 8:16], s_cut[:, c, :]))
                own.settle()
                cf = cand[:, :, :].rearrange("p a b -> p (a b)")
                own.after(dve.tensor_copy(topf[:, :, :], topi[:, :, :]))
                own.after(dve.max(cv[:, 0:8], cf))
                own.settle()
                own.after(dve.match_replace(cand2[:, :], cv[:, 0:8], cf, LOWEST))
                own.after(dve.max_index(ci[:, 0:8], cv[:, 0:8], cf))
                own.after(dve.tensor_scalar(ncv[:, 0:1], cv[:, 0:1], -1.0, None, ALU.mult))
                own.settle()
                own.after(dve.max(cv[:, 8:16], cand2[:, :]))
                own.settle()
                dve.max_index(ci[:, 8:16], cv[:, 8:16], cand2[:, :]).then_inc(cv_ready, 1)
                dve.wait_ge(cv_ready, step + 1)
                own.after(dve.tensor_scalar(cij[:, 0, :], ci[:, :], 4, None,
                                            ALU.logical_shift_right))
                own.after(dve.tensor_scalar(cij[:, 1, :], ci[:, :], 15, None, ALU.bitwise_and))
                own.settle()
                own.after(dve.tensor_copy(cijf[:, :, :], cij[:, :, :]))
                own.settle()
                own.after(dve.tensor_tensor(
                    onehot[:, :, :, :].rearrange("p c k n -> p (c k) n"),
                    iota16[:, :].unsqueeze(1).to_broadcast([P, 2 * TOPK, TOPK]),
                    cijf[:, :, :].rearrange("p c k -> p (c k)").unsqueeze(2)
                    .to_broadcast([P, 2 * TOPK, TOPK]), ALU.is_equal))
                own.settle()
                own.after(dve.tensor_tensor(
                    onehot[:, :, :, :], onehot[:, :, :, :],
                    topf[:, :, :].unsqueeze(2).to_broadcast([P, 2, TOPK, TOPK]), ALU.mult))
                own.settle()
                own.after(dve.tensor_reduce(pick[:, :, :], onehot[:, :, :, :], AX, ALU.add))
                own.settle()
                own.after(dve.scalar_tensor_tensor(idx_f[:, :], pick[:, 0, :], float(NK),
                                                   pick[:, 1, :], ALU.mult, ALU.add))
                dve.wait_ge(gate_exp, step + 1)
                own.after(dve.reciprocal(esum[:, 1:2], esum[:, 0:1]))
                own.settle()
                dve.tensor_scalar(gate[:, par_, :], gexp[:, :], esum[:, 1:2], None, ALU.mult)
                dve.wait_ge(v_free, step * TOPK - TOPK + G if not isinstance(step, int) else G)
                dve.tensor_scalar(idx_u[:, par_, :], idx_f[:, :], table_base[:, 0:1], None,
                                  ALU.add).then_inc(idx_ready, 1)
                dve.sem_clear(pick_step)

            def dots(step, par_, half, tile):
                for r in range(G):
                    dve.wait_ge(u_loaded[r], (step * 2 + half + 1) * 16)
                    k = half * G + r
                    dve.tensor_tensor_reduce(
                        out=urow[:, r, :], in0=urow[:, r, :], in1=xn[:, tile, :], scale=1.0,
                        scalar=0.0, op0=ALU.mult, op1=ALU.add,
                        accum_out=hid[:, par_, k:k + 1]).then_inc(u_free, 1)
                dve.wait_ge(gelu_ready, step * 2 + half + 1)
                c = slice(half * G, half * G + G)
                dve.tensor_tensor(wgt[:, par_, c], gelu[:, par_, c], gate[:, par_, c], ALU.mult
                                  ).then_inc(wgt_ready, 1)

            def pair_of(pair, tile, is_last=False):
                for par_ in range(2):
                    step = pair * 2 + par_
                    dots(step, par_, 0, tile)
                    if not (is_last and par_):
                        pick_experts(step + 1, 1 - par_)
                    dots(step, par_, 1, tile)

            dve.wait_ge(const_ready, 1)
            with dve.Fori(0, DEPTH) as layer:
                own = Steps(dve, dve_step)
                dve.wait_ge(first_T, 1)
                dve.tensor_copy(par[:, :], ps[:, 7, 0:76]).then_inc(par_ready, 1)
                dve.wait_ge(first_T, 3)
                hv = halo[:, :, :].rearrange("p f (b t) -> p f b t", b=NB)
                for f in range(NC3):
                    ins = dve.tensor_copy(hv[:, f, :, 0:CONV_W - 1], ps[:, 4, 24 * f:24 * (f + 1)]
                                          .rearrange("p (b j) -> p b j", b=NB))
                ins.then_inc(hist_ready, 1)
                norm(0, own)
                dve.wait_ge(small_loaded, 80)
                dve.wait_ge(unit_out, 2)
                own.after(dve.tensor_tensor(ypos[:, :, :], ba[:, :, HD:2 * HD],
                                            ad[:, 1, :].unsqueeze(1).to_broadcast([P, TILES, HD]),
                                            ALU.add))
                own.settle()
                dve.sem_inc(y_in, 1)
                dve.wait_ge(gx_ready, 1)
                own.after(dve.scalar_tensor_tensor(gb[:, :, :], gb[:, :, :], 0.0, q_mid[:, :, :],
                                                   ALU.min, ALU.subtract))
                own.settle()
                for r in range(2):
                    own.after(dve.tensor_tensor_scan(gb[:, r, :], reset[:, :], gb[:, r, :], 0.0,
                                                     ALU.mult, ALU.add))
                own.settle()
                for c0, c1, size in ((0, SEQ, GLA_CHUNK), (SEQ, NT, TS)):
                    n, mid = (c1 - c0) // size, size // 2 - 1
                    for r in range(2):
                        b3 = gb[:, r, c0:c1].rearrange("p (c t) -> p c t", t=size)
                        for to, at in ((q_mid, mid), (k_last, size - 1)):
                            ins = dve.tensor_tensor(
                                to[:, r, c0:c1].rearrange("p (c t) -> p c t", t=size), b3,
                                b3[:, :, at:at + 1].to_broadcast([P, n, size]), ALU.subtract)
                ins.then_inc(gl_args, 1)
                dve.wait_ge(soft_ready, 1)
                own.after(dve.scalar_tensor_tensor(soft[:, :, :], ypos[:, :, :], 0.0, soft[:, :, :],
                                                   ALU.max, ALU.add))
                own.settle()
                own.after(dve.tensor_scalar(soft[:, :, :], soft[:, :, :], -1.0, None, ALU.mult))
                own.settle()
                dve.tensor_tensor(g_tok[:, :, :], soft[:, :, :],
                                  ad[:, 0, :].unsqueeze(1).to_broadcast([P, TILES, HD]), ALU.mult
                                  ).then_inc(g_ready, 1)
                dve.wait_ge(gl_exps, 1)
                q1, k1 = q1k1[:, 0:2, :], q1k1[:, 2:4, :]
                scale = float(DK) ** -0.5
                dve.tensor_tensor(k_mid[:, :, :], k_mid[:, :, :], k1, ALU.mult)
                dve.tensor_tensor(k_last[:, :, :], k_last[:, :, :], k1, ALU.mult)
                dve.scalar_tensor_tensor(q_all[:, :, :], q1, scale, e_all[:, :, :], ALU.mult,
                                         ALU.mult)
                dve.scalar_tensor_tensor(q_mid[:, :, :], q1, scale, q_mid[:, :, :], ALU.mult,
                                         ALU.mult).then_inc(gl_ops, 1)
                for f in range(NC3):
                    dve.wait_ge(unit_out, U_QKV + f + 1)
                    hf = hv[:, f, :, :]
                    out_p = qkvc[:, f, 0:SEQ]
                    out_s = qkvc[:, f, SEQ:NT].rearrange("p (b t) -> p b t", t=TS)
                    for d in range(CONV_W):
                        j = CONV_W - 1 - d
                        w = par[:, PAR_CONV + NC3 * j + f:PAR_CONV + NC3 * j + f + 1]
                        if d == 0:
                            own.after(dve.tensor_scalar(out_p, raw[:, f, 0:SEQ], w, None, ALU.mult))
                            own.after(dve.tensor_scalar(out_s, hf[:, :, j:j + TS], w, None, ALU.mult))
                        else:
                            own.after(dve.scalar_tensor_tensor(
                                out_p[:, d:], raw[:, f, 0:SEQ - d], w, out_p[:, d:], ALU.mult,
                                ALU.add))
                            own.after(dve.scalar_tensor_tensor(
                                out_s, hf[:, :, j:j + TS], w, out_s, ALU.mult, ALU.add))
                        own.settle()
                    dve.sem_inc(conv_done, 1)
                dve.tensor_copy(tail[:, :, 3:27].rearrange("p f (b j) -> p f b j", b=NB),
                                hv[:, :, :, TS:TS + 3])
                dve.tensor_copy(tail[:, :, 0:3], raw[:, :, SEQ - 3:SEQ]).then_inc(tail_ready, 1)
                dve.wait_ge(tail_ready, 1)

                dve.wait_ge(unit_mm, len(units))
                flat = "p a b -> p (a b)"
                own.settle()
                for s_ in range(2):
                    dve.tensor_scalar(k_one[:, s_, :], k_mid[:, :, :].rearrange(flat),
                                      half_of[:, s_:s_ + 1], None, ALU.mult)
                    ins = dve.tensor_scalar(q_one[:, s_, :], q_all[:, :, :].rearrange(flat),
                                            half_of[:, s_:s_ + 1], None, ALU.mult)
                ins.then_inc(one_ready, 1)
                for i in range(TILES):
                    R = ROWS[i]
                    dve.wait_ge(att_mm, i + 1)
                    dve.tensor_tensor(
                        attT[0:R, 512 * i:512 * (i + 1)].rearrange("p (a b) -> p a b", b=P)[:, :, 0:R],
                        heads(i, R, R), over_heads(incl64 if i < 2 else incl8, R), ALU.mult
                    ).then_inc(att_ready, 1)
                for c in range(SEQ // GLA_CHUNK):
                    dve.wait_ge(gU_mm, c + 1)
                    at = GLA_CHUNK * (c + 1) - 1
                    for r in range(2):
                        for s_ in range(2):
                            rows = slice(64 * s_, 64 * s_ + 64)
                            u = ps[rows, 6 + c % 2, 256 * r + P * s_:256 * r + P * s_ + P]
                            if c == 0:
                                ins = dve.tensor_copy(gS[rows, r, :], u)
                            else:
                                ins = dve.scalar_tensor_tensor(
                                    gS[rows, r, :], gS[rows, r, :], e_all[rows, r, at:at + 1], u,
                                    ALU.mult, ALU.add)
                    ins.then_inc(gS_ready, 1)
                dve.wait_ge(gs_decayed, 1)
                gs4 = gSs[:, :, :].rearrange("p (b r) v -> p b r v", r=2)
                for n in range(8):
                    hd, half = n // 2, n % 2
                    rows = slice(64 * (hd % 2), 64 * (hd % 2) + 64)
                    s_ = gs4[rows, 4 * half:4 * half + 4, hd // 2, :]
                    dve.wait_ge(gs_mm, n + 1)
                    dve.tensor_tensor(s_, s_, ps[rows, n % 3, :].rearrange("p (b v) -> p b v", b=4),
                                      ALU.add).then_inc(gs_add, 1)
                out_norm(0, own)

                dve.wait_ge(l2_sum, 1)
                for m, b in enumerate((0, 1, 2, 6, 7)):
                    ins = dve.tensor_scalar(l2sq[:, 512 * m:512 * (m + 1)], bank(b), EPS, None,
                                            ALU.add)
                ins.then_inc(l2_var, 1)
                dve.wait_ge(l2_std, 1)
                own.after(dve.reciprocal(l2sq[:, :], l2sq[:, :]))
                own.settle()
                inv = l2sq[:, :].rearrange("p (a b) -> p a b", b=NT)
                dve.scalar_tensor_tensor(qkvc[:, 0:NH, :], qkvc[:, 0:NH, :], float(P) ** -0.5,
                                         inv[:, 0:NH, :], ALU.mult, ALU.mult)
                own.after(dve.tensor_tensor(qkvc[:, NH:2 * NH, :], qkvc[:, NH:2 * NH, :],
                                            inv[:, NH:2 * NH, :], ALU.mult))
                own.settle()
                dve.sem_inc(qk_ready, 1)
                dve.wait_ge(gst_mm, 1)
                dve.tensor_copy(gst[:, 0:2, :], ps[:, 6, 0:16].rearrange("p (i n) -> p i n", n=8))
                own.after(dve.tensor_copy(gst[0:64, 2, :], ps[0:64, 6, 16:24]))
                own.settle()
                dve.tensor_tensor(kds[:, :, :], gst[:, :, HD:2 * HD], gst[:, :, 0:HD], ALU.subtract
                                  ).then_inc(gst_ready, 1)
                for i in range(TILES):
                    R = ROWS[i]
                    dve.wait_ge(bB_mm, i + 1)
                    for hd in range(NH):
                        src, b_row = heads(i, R, R)[:, hd, :], gst[0:R, i, hd:hd + 1]
                        dve.tensor_scalar(temp(i, 0, R)[:, hd, 0:R], src, b_row, 0.0, ALU.subtract,
                                          ALU.max)
                        ins = dve.tensor_scalar(temp(i, 1, R)[:, hd, 0:R], src, b_row, 0.0,
                                                ALU.subtract, ALU.min)
                    ins.then_inc(dargs, 1)
                for done in stored[0:4]:
                    dve.wait_ge(done, 16)
                for i in range(TILES):
                    R = ROWS[i]
                    dec = temp(i, 0, R)[:, :, 0:R]
                    P1, low = slot(SA[i], R)[:, :, 0:R], (low128 if i < 2 else low8)
                    dve.wait_ge(dexp, i + 1)
                    for hd in range(NH):
                        own.after(dve.scalar_tensor_tensor(
                            dec[:, hd, :], dec[:, hd, :], beta[0:R, i, hd:hd + 1], low[0:R, 0:R],
                            ALU.mult, ALU.mult))
                    own.settle()
                    dve.wait_ge(G_mm, i + 1)
                    if i < 2:
                        own.after(dve.tensor_tensor(dec, heads(3 + i, R, R), dec, ALU.mult))
                        own.settle()
                        own.after(dve.tensor_tensor(P1, dec, over_heads(sub16, R), ALU.mult))
                        own.settle()
                        own.after(dve.tensor_tensor(slot(SO[i])[:, :, :], dec, P1, ALU.subtract))
                    else:
                        own.after(dve.tensor_tensor(P1, heads(3 + i, R, R), dec, ALU.mult))
                    own.settle()
                    dve.sem_inc(P1_ready, 1)
                for i in range(TILES):
                    R = ROWS[i]
                    d1 = temp(i, 1, R)[:, :, 0:R]
                    own.after(dve.tensor_tensor(d1, d1, over_heads(incl128 if i < 2 else incl8, R),
                                                ALU.mult))
                    own.settle()
                    dve.wait_ge(qk_mm, i + 1)
                    dve.tensor_tensor(slot(SQK[i], R)[:, :, 0:R], heads(i, R, R), d1, ALU.mult
                                      ).then_inc(qkT_ready, 1)
                for i in range(TILES):
                    R = ROWS[i]
                    dve.wait_ge(P1T_out, i + 1)
                    dve.scalar_tensor_tensor(slot(SF[i], R)[:, :, 0:R], slot(SB[i], R)[:, :, 0:R], -1.0,
                                             over_heads(ident, R), ALU.mult, ALU.add
                                             ).then_inc(F0_ready, 1)
                n = 0
                for k, (to, _, _, who) in enumerate(solve):
                    for i in solve_tiles(k):
                        n += 1
                        R = ROWS[i]
                        src, t = heads(i + 3 * (k % 2), R, R), slot(to[i], R)[:, :, 0:R]
                        if who == "act":
                            continue
                        dve.wait_ge(solve_mm, n)
                        if k == N_T:
                            own.after(dve.scalar_tensor_tensor(
                                slot(SH[i])[:, :, :], src, -1.0, over_heads(ident, R), ALU.mult,
                                ALU.add))
                        if who == "+":
                            dve.tensor_tensor(t, src, t, ALU.add).then_inc(solve_dve, 1)
                        else:
                            dve.tensor_copy(t, src).then_inc(solve_dve, 1)

                for i in range(TILES):
                    R = ROWS[i]
                    r_, b_ = temp(i, 1, R), per_head(beta[0:R, i, :], R)
                    v_ = v2tok[0:R, i, :].rearrange("p (a b) -> p a b", b=P)
                    if i > 0:
                        dve.wait_ge(kS_mm, i)
                        own.after(dve.tensor_tensor(r_, heads(0, R), per_head(eb[0:R, i, 0:HD], R),
                                                    ALU.mult))
                        own.settle()
                        own.after(dve.tensor_tensor(r_, v_, r_, ALU.subtract))
                        own.settle()
                        v_ = r_
                    else:
                        dve.wait_ge(gst_exp, 1)
                    dve.tensor_tensor(r_, v_, b_, ALU.mult).then_inc(r_ready, 1)
                    if i < 2:
                        dve.wait_ge(dU_mm, i + 1)
                        for hd in range(NH):
                            u = heads(6)[:, hd, :]
                            if i == 0:
                                ins = dve.tensor_copy(dS[:, hd, :], u)
                            else:
                                ins = dve.scalar_tensor_tensor(
                                    dS[:, hd, :], dS[:, hd, :], eb[:, i, HD + hd:HD + hd + 1], u,
                                    ALU.mult, ALU.add)
                        ins.then_inc(dS_ready, 1)
                dve.wait_ge(ds_decayed, 1)
                for n in range(8):
                    hd, half = n // 2, n % 2
                    s_ = dSs[:, 4 * half:4 * half + 4, hd, :]
                    dve.wait_ge(ds_mm, n + 1)
                    dve.tensor_tensor(s_, s_, bank(n % 3).rearrange("p (b v) -> p b v", b=4),
                                      ALU.add).then_inc(ds_add, 1)
                out_norm(1, own)

                for n in range(12):
                    m, i = n // 3, n % 3
                    t = h[:, i, WCOLS * m:WCOLS * (m + 1)]
                    dve.wait_ge(mix_mm, n + 1)
                    dve.tensor_tensor(t, t, bank((0, 1, 2, 7)[n % 4], cols=WCOLS), ALU.add
                                      ).then_inc(mix_add, 1)
                norm(1, own)
                for n in range(4):
                    dve.wait_ge(key_T, n + 1)
                    dve.tensor_copy(keysT[:, 4 * n:4 * n + 4, :].rearrange("p a b -> p (a b)"),
                                    bank(6 + n % 2)).then_inc(key_out, 1)
                dve.sem_inc(u_free, G)
                dve.wait_ge(score_out, 12)
                pick_experts(0, 0)
                for tile in range(2):
                    with dve.Fori(HP // 2 * tile, HP // 2 * (tile + 1)) as pair:
                        pair_of(pair, tile)
                pair_of(HP, 2)
                pair_of(HP + 1, 2, is_last=True)
                dve.wait_ge(v_free, G + NSTEP * TOPK)
                for i in range(TILES):
                    dve.tensor_tensor(h[:, i, :], h[:, i, :],
                                      ps[:, 2 * i:2 * i + 2, :].rearrange("p a b -> p (a b)"),
                                      ALU.add).then_inc(h_added, 1)
                norm(2, own)
                for n in range(12):
                    m, i = n // 3, n % 3
                    t, g_ = h[:, i, WCOLS * m:WCOLS * (m + 1)], sig[:, n % 2, :]
                    dve.wait_ge(ple_sig, n + 1)
                    own.after(dve.tensor_tensor(g_, g_, ps[:, 4 + n % 4, WCOLS:2 * WCOLS], ALU.mult))
                    own.settle()
                    dve.tensor_tensor(t, t, g_, ALU.add).then_inc(ple_done, 1)
                dve.tensor_scalar(table_base[:, :], table_base[:, :], float(NEXP), None, ALU.add)
                meet(dve, layer)
            dve.wait_ge(fin_sq, 3)
            dve.tensor_scalar(ssq[:, 0:3], ssq[:, 0:3], 1.0 / D, EPS, ALU.mult, ALU.add
                              ).then_inc(fin_var, 1)
            dve.wait_ge(fin_std, 1)
            dve.wait_ge(fin_row, 16)
            dve.reciprocal(rstd[:, 0:3], rstd[:, 0:3]).then_inc(fin_step, 1)
            dve.wait_ge(fin_step, 1)
            for i in range(TILES):
                dve.scalar_tensor_tensor(xn[:, i, :], h[:, i, :], rstd[:, i:i + 1], gain_row[:, :],
                                         ALU.mult, ALU.mult).then_inc(y_ready, 1)

        @block.tensor
        def _(pe):
            def mm(out, lhsT, rhs, start=True, stop=True):
                return pe.matmul(out, lhsT, rhs, start=start, stop=stop, skip_group_check=True)

            def transpose_rows(use):
                pe.wait_ge(xn_ready, TILES * (use + 1))
                for k in range(KD):
                    n = KD * use + k
                    if k >= 2:
                        pe.wait_ge(aT_ready, n - 1)
                    for i in range(TILES):
                        ins = pe.transpose(ps[:, k % 2, P * i:P * (i + 1)],
                                           xn[:, i, P * k:P * (k + 1)], ident[:, :])
                    ins.then_inc(xT_done, 1)
                pe.wait_ge(aT_ready, KD * (use + 1))

            def arrived(n):
                pe.wait_ge(w_loaded[n % RING], 16 * (n // RING + 1))

            def product(out, n, c, cols, moving):
                for k in range(KD):
                    ins = mm(out, wring[:, n % RING, k, c:c + cols], moving(k), k == 0, k == KD - 1)
                return ins

            def out_sums(which):
                sq = gosq if which == 0 else dosq
                for i in range(TILES):
                    R = ROWS[i]
                    pe.wait_ge(on_sq, TILES * which + i + 1)
                    if i == 2:
                        pe.wait_ge(on_var, TILES * which + 1)
                    mm(ps[:, 6 + i % 2, 0:NH * R], ones[:, :], sq[:, 512 * i:512 * i + NH * R]
                       ).then_inc(on_sum, 1)

            pe.wait_ge(const_ready, 1)
            with pe.Fori(0, DEPTH) as layer:
                pe.wait_ge(par_loaded, 7 * 16)
                pe.transpose(ps[:, 7, 0:76], par_rows[0:76, :], ident[0:76, 0:76]).then_inc(first_T, 1)
                pe.wait_ge(ptok_loaded, 48)
                for k in range(KP):
                    for i in range(TILES):
                        ins = pe.transpose(ps[:, 5 + k, P * i:P * (i + 1)],
                                           ptok[:, i, P * k:P * (k + 1)], ident[:, :])
                ins.then_inc(first_T, 1)
                pe.wait_ge(hist_loaded, 16)
                for f in range(NC3):
                    ins = pe.transpose(ps[:, 4, 24 * f:24 * (f + 1)], hist_rows[:, P * f:P * (f + 1)],
                                       ident[0:24, 0:24])
                ins.then_inc(first_T, 1)
                transpose_rows(0)

                pe.wait_ge(small_loaded, 80)
                pe.wait_ge(hist_ready, 1)
                pe.wait_ge(pT_ready, 1)
                for n, (name, f, blk) in enumerate(units):
                    b = 2 + n % 4
                    if n >= 4:
                        pe.wait_ge(unit_out, n - 3)
                    if blk is not None:
                        arrived(blk)
                    tokens = lambda k: aT[:, k, 0:NT]
                    if name == "lr":
                        for k in range(KD):
                            ins = mm(ps[0:RANK, b, 0:NT], w_lrba[:, k, 0:RANK], tokens(k), k == 0,
                                     k == KD - 1)
                    elif name == "ba":
                        for i in range(TILES):
                            R = ROWS[i]
                            for k in range(KD):
                                ins = mm(ps[0:R, b, 8 * i:8 * i + 8], aT[:, k, COL[i]:COL[i] + R],
                                         w_lrba[:, k, RANK:24], k == 0, k == KD - 1)
                    elif name == "v1":
                        m, i = f
                        R = ROWS[i]
                        for k in range(KD):
                            ins = mm(ps[0:R, b, 0:WCOLS], aT[:, k, COL[i]:COL[i] + R],
                                     wring[:, blk % RING, k, :], k == 0, k == KD - 1)
                    else:
                        ins = product(ps[:, b, 0:NT], blk, P * (f % 2), P, tokens)
                    ins.then_inc(unit_mm, 1)
                    if blk is not None and (n + 1 == len(units) or units[n + 1][2] != blk):
                        pe.wait_ge(unit_mm, n + 1)
                        pe.sem_inc(block_used, 1)
                    if n == 5:
                        pe.wait_ge(unit_out, 1)
                        for r in range(2):
                            ins = mm(ps[:, 6 + r, 0:NT], w_up[:, P * r:P * (r + 1)], lrT[:, :])
                        ins.then_inc(gate_mm, 1)

                pe.wait_ge(gl_ops, 1)
                for i in range(TILES):
                    R = ROWS[i]
                    for r in range(2):
                        c = 256 * (i % 2) + P * r
                        ins = pe.transpose(ps[0:R, 6 + i // 2, c:c + P],
                                           k_last[:, r, COL[i]:COL[i] + R], ident[:, :])
                ins.then_inc(kd_T, 1)

                def one(t, hd):
                    return t[:, hd % 2, NT * (hd // 2):NT * (hd // 2 + 1)]

                pe.wait_ge(one_ready, 1)
                pe.wait_ge(unit_out, len(units))
                for i in range(TILES):
                    R, c = ROWS[i], slice(COL[i], COL[i] + ROWS[i])
                    for hd in range(NH):
                        ins = mm(heads(i, R, R)[:, hd, :], one(k_one, hd)[:, c], q_mid[:, hd // 2, c])
                    ins.then_inc(att_mm, 1)
                for i in range(TILES):
                    R = ROWS[i]
                    pe.wait_ge(att_ready, i + 1)
                    for hd in range(NH):
                        mm(heads(3 + i, P, R)[:, hd, :], v1[0:R, i, P * hd:P * (hd + 1)],
                           attT[0:R, 512 * i + P * hd:512 * i + P * hd + R], hd == 0, False)
                pe.wait_ge(k_tok_ready, 1)
                for c in range(SEQ // GLA_CHUNK):
                    i, s_ = c // 2, slice(64 * (c % 2), 64 * (c % 2) + 64)
                    if c > 0:
                        pe.wait_ge(gS_ready, c)
                        for hd in range(NH):
                            ins = mm(heads(3 + i)[:, hd, s_], gS[:, hd // 2, :],
                                     one(q_one, hd)[:, 64 * c:64 * c + 64], False, False)
                        if c % 2:
                            ins.then_inc(go_mm, 1)
                    for r in range(2):
                        ins = mm(ps[:, 6 + c % 2, 256 * r:256 * r + 256],
                                 k_tok[s_, i, P * r:P * (r + 1)], v1[s_, i, 256 * r:256 * r + 256])
                    ins.then_inc(gU_mm, 1)
                pe.wait_ge(gSs_loaded, 16)
                for b in range(NB):
                    c = slice(SEQ + TS * b, SEQ + TS * (b + 1))
                    for hd in range(NH):
                        ins = mm(heads(5)[:, hd, TS * b:TS * (b + 1)], gSs[:, 2 * b + hd // 2, :],
                                 one(q_one, hd)[:, c], False, False)
                ins.then_inc(go_mm, 1)
                pe.wait_ge(gvm_ready, 1)
                for n in range(8):
                    hd, half = n // 2, n % 2
                    if n >= 3:
                        pe.wait_ge(gs_add, n - 2)
                    mm(bank(n % 3), k_tok[0:64, 2, P * (hd // 2):P * (hd // 2 + 1)],
                       vmask[:, hd, 4 * half:4 * half + 4, :]).then_inc(gs_mm, 1)
                pe.wait_ge(gS_ready, 4)
                out_sums(0)
                pe.wait_ge(tail_ready, 1)
                pe.wait_ge(gs_add, 8)
                for f in range(NC3):
                    ins = pe.transpose(ps[0:27, f // 4, P * (f % 4):P * (f % 4 + 1)], tail[:, f, :],
                                       ident[:, :])
                ins.then_inc(first_T, 1)
                pe.wait_ge(l2_sq, 1)
                pe.wait_ge(conv_rows_ready, 1)
                pe.wait_ge(on_var, 3)
                for m, b in enumerate((0, 1, 2, 6, 7)):
                    ins = mm(bank(b), ones[:, :], l2sq[:, 512 * m:512 * (m + 1)])
                ins.then_inc(l2_sum, 1)
                pe.wait_ge(o_ready, 3)
                for i in range(TILES):
                    c = slice(COL[i], COL[i] + ROWS[i])
                    for hd in range(NH):
                        ins = pe.transpose(heads(3 + i, ROWS[i])[:, hd, :], qkvc[:, 2 * NH + hd, c],
                                           ident[:, :])
                    ins.then_inc(v2_T, 1)
                pe.wait_ge(qk_ready, 1)
                for i in range(TILES):
                    c = slice(COL[i], COL[i] + ROWS[i])
                    for hd in range(NH):
                        ins = pe.transpose(heads(i, ROWS[i])[:, hd, :], qkvc[:, NH + hd, c],
                                           ident[:, :])
                    ins.then_inc(k2_T, 1)
                pe.wait_ge(g_ready, 1)
                for i in range(TILES):
                    R = ROWS[i]
                    incl, same = (incl128, ones) if i < 2 else (incl8, same8)
                    mm(ps[0:R, 6, 8 * i:8 * i + 4], incl[0:R, 0:R], g_tok[0:R, i, :])
                    ins = mm(ps[0:R, 6, 8 * i + 4:8 * i + 8], same[0:R, 0:R], g_tok[0:R, i, :])
                ins.then_inc(gst_mm, 1)
                for i in range(TILES):
                    R = ROWS[i]
                    incl = incl128 if i < 2 else incl8
                    pe.wait_ge(k2tok_ready, i + 1)
                    for hd in range(NH):
                        ins = mm(heads(i, P, R)[:, hd, :],
                                 g_tok[0:R, i, hd:hd + 1].to_broadcast([R, P]), incl[0:R, 0:R])
                    ins.then_inc(bB_mm, 1)
                for i in range(TILES):
                    R, c = ROWS[i], slice(COL[i], COL[i] + ROWS[i])
                    pe.wait_ge(v2tok_ready, i + 1)
                    for hd in range(NH):
                        ins = mm(heads(3 + i, R, R)[:, hd, :], qkvc[:, NH + hd, c],
                                 qkvc[:, NH + hd, c])
                    ins.then_inc(G_mm, 1)
                for i in range(TILES):
                    R, c = ROWS[i], slice(COL[i], COL[i] + ROWS[i])
                    pe.wait_ge(dexp, i + 1)
                    for hd in range(NH):
                        ins = mm(heads(i, R, R)[:, hd, :], qkvc[:, NH + hd, c], qkvc[:, hd, c])
                    ins.then_inc(qk_mm, 1)
                for i in range(TILES):
                    R = ROWS[i]
                    pe.wait_ge(P1_ready, i + 1)
                    for hd in range(NH):
                        ins = pe.transpose(heads(3 + i, R, R)[:, hd, :],
                                           slot(SA[i], R)[:, hd, 0:R], ident[0:R, 0:R])
                    ins.then_inc(P1T_mm, 1)
                for k, (to, left, right, who) in enumerate(solve):
                    for i in solve_tiles(k):
                        R = ROWS[i]
                        if k == 0:
                            pe.wait_ge(P1T_out, i + 1)
                            pe.wait_ge(F0_ready, i + 1)
                            pe.wait_ge(qkT_ready, i + 1)
                        else:
                            by = solve[k - 1][3]
                            pe.wait_ge(solve_act if by == "act" else solve_dve,
                                       evacuations(k - 1, by) + i + 1)
                        for hd in range(NH):
                            ins = mm(heads(i + 3 * (k % 2), R, R)[:, hd, :],
                                     slot(left[i], R)[:, hd, 0:R], slot(right[i], R)[:, hd, 0:R])
                        ins.then_inc(solve_mm, 1)
                pe.wait_ge(solve_act, evacuations(len(solve), "act"))
                pe.wait_ge(solve_dve, evacuations(len(solve), "dve"))

                pe.wait_ge(kd_ready, 1)
                pe.wait_ge(qd_ready, 1)
                for i in range(TILES):
                    R, c = ROWS[i], slice(COL[i], COL[i] + ROWS[i])
                    if i == 1:
                        pe.wait_ge(dS_ready, 1)
                        for hd in range(NH):
                            ins = mm(heads(0)[:, hd, :], qkvc[:, NH + hd, c], dS[:, hd, :])
                        ins.then_inc(kS_mm, 1)
                    if i == 2:
                        pe.wait_ge(dSs_loaded, 16)
                        for b in range(NB):
                            for hd in range(NH):
                                ins = mm(ps[:, 7, 64 * hd + TS * b:64 * hd + TS * (b + 1)],
                                         dSs[:, b, hd, :],
                                         qkvc[:, NH + hd, SEQ + TS * b:SEQ + TS * (b + 1)])
                        ins.then_inc(kST_mm, 1)
                        pe.wait_ge(kST_ready, 1)
                        for hd in range(NH):
                            ins = pe.transpose(heads(0, 64)[:, hd, :], kST[:, hd, :], ident[:, :])
                        ins.then_inc(kS_mm, 1)
                    pe.wait_ge(r_ready, i + 1)
                    if i < 2:
                        for hd in range(NH):
                            ins = mm(heads(1)[:, hd, :], slot(SF[i])[:, hd, :], temp(i, 1)[:, hd, :])
                        ins.then_inc(y_mm, 1)
                        pe.wait_ge(y_out, i + 1)
                    if i > 0:
                        pe.wait_ge(vn_ready, i)
                    for hd in range(NH):
                        left, right = (slot(SH[i]), temp(i, 0)) if i < 2 else (slot(SF[i], 64),
                                                                            temp(i, 1, 64))
                        ins = mm(heads(2, R)[:, hd, :], left[:, hd, 0:R], right[:, hd, :])
                    ins.then_inc(vn_mm, 1)
                    if i == 1:
                        for hd in range(NH):
                            mm(heads(3 + i)[:, hd, :], dS[:, hd, :], qkvc[:, hd, c], hd == 0, False)
                    if i == 2:
                        for b in range(NB):
                            for hd in range(NH):
                                mm(heads(5)[:, hd, TS * b:TS * (b + 1)], dSs[:, b, hd, :],
                                   qkvc[:, hd, SEQ + TS * b:SEQ + TS * (b + 1)],
                                   b == 0 and hd == 0, False)
                    pe.wait_ge(vn_ready, i + 1)
                    for hd in range(NH):
                        ins = mm(heads(3 + i, P, R)[:, hd, :], vnew(i, R)[:, hd, :],
                                 slot(SQK[i], R)[:, hd, 0:R], i == 0 and hd == 0, False)
                    ins.then_inc(do_mm, 1)
                    if i < 2:
                        if i == 1:
                            pe.wait_ge(dS_ready, 1)
                        for hd in range(NH):
                            ins = mm(heads(6)[:, hd, :], kd[:, 512 * i + P * hd:512 * i + P * (hd + 1)],
                                     vnew(i)[:, hd, :])
                        ins.then_inc(dU_mm, 1)
                pe.wait_ge(dvm_ready, 1)
                for n in range(8):
                    hd, half = n // 2, n % 2
                    if n >= 3:
                        pe.wait_ge(ds_add, n - 2)
                    mm(bank(n % 3), kd[0:64, 1024 + P * hd:1024 + P * (hd + 1)],
                       vmask[:, hd, 4 * half:4 * half + 4, :]).then_inc(ds_mm, 1)
                pe.wait_ge(dS_ready, 2)
                out_sums(1)

                pe.wait_ge(o_ready, 6)
                pe.wait_ge(ds_add, 8)
                for n in range(12):
                    m, i = n // 3, n % 3
                    if i == 0:
                        arrived(B_OUT + m)
                    if n >= 4:
                        pe.wait_ge(mix_add, n - 3)
                    for k in range(KD):
                        ins = mm(bank((0, 1, 2, 7)[n % 4], cols=WCOLS), oall[:, k, P * i:P * (i + 1)],
                                 wring[:, (B_OUT + m) % RING, k, :], k == 0, k == KD - 1)
                    ins.then_inc(mix_mm, 1)
                    if i == 2:
                        pe.wait_ge(mix_mm, n + 1)
                        pe.sem_inc(block_used, 1)

                transpose_rows(1)
                pe.wait_ge(keys_loaded, 16)
                for n in range(4):
                    if n >= 2:
                        pe.wait_ge(key_out, n - 1)
                    for m in range(4):
                        ins = pe.transpose(ps[:, 6 + n % 2, P * m:P * (m + 1)],
                                           keys_n[:, 4 * n + m, :], ident[:, :])
                    ins.then_inc(key_T, 1)
                for n in range(2 * HP):
                    blk = B_PQ + n // 2
                    arrived(blk)
                    if n >= 4:
                        pe.wait_ge(q_out, n - 3)
                    product(ps[:, 2 + n % 4, 0:NT], blk, P * (n % 2), P, lambda k: aT[:, k, 0:NT]
                            ).then_inc(q_mm, 1)
                    if n % 2:
                        pe.wait_ge(q_mm, n + 1)
                        pe.sem_inc(block_used, 1)
                pe.wait_ge(q_out, 2 * HP)
                pe.wait_ge(key_out, 4)
                for n in range(12):
                    i, m = n // 4, n % 4
                    if n >= 4:
                        pe.wait_ge(score_out, n - 3)
                    for j in range(4):
                        f = 4 * m + j
                        ins = mm(ps[:, (6 + n % 4) % 8, P * j:P * (j + 1)],
                                 qT[:, f, P * i:P * (i + 1)], keysT[:, f, :])
                    ins.then_inc(score_mm, 1)

                pe.wait_ge(score_out, 12)
                for b in range(6):
                    mm(bank(b), zero[:, :], zero[:, :].unsqueeze(1).to_broadcast([P, 4, P]))
                pe.sem_inc(v_free, G)

                def add_pair(pair, tile):
                    for par_ in range(2):
                        for half in range(2):
                            step = pair * 2 + par_
                            for r in range(G):
                                pe.wait_ge(v_loaded[r], (step * 2 + half + 1) * 16)
                                pe.wait_ge(diag_ready, step * TOPK + half * G + r + 1)
                                for m in range(2):
                                    ins = mm(bank(2 * tile + m), diag[:, r, :],
                                             vrow[:, r, BANK * m:BANK * (m + 1)], False, False)
                                ins.then_inc(v_free, 1)

                for tile in range(2):
                    with pe.Fori(HP // 2 * tile, HP // 2 * (tile + 1)) as pair:
                        add_pair(pair, tile)
                with pe.Fori(HP, NSTEP // 2) as pair:
                    add_pair(pair, 2)

                transpose_rows(2)
                pe.wait_ge(wproj_loaded, 16)
                for n in range(12):
                    m, i = n // 3, n % 3
                    b = 4 + n % 4
                    blk = B_PLE + m
                    if i == 0:
                        arrived(blk)
                    if n >= 4:
                        pe.wait_ge(ple_done, n - 3)
                    for k in range(KD):
                        mm(ps[:, b, 0:WCOLS], aT[:, k, P * i:P * (i + 1)],
                           wring[:, blk % RING, k, :], k == 0, False)
                    mm(ps[:, b, 0:WCOLS], ones[0:1, :], bias_row[:, WCOLS * m:WCOLS * (m + 1)],
                       False, True)
                    for k in range(KP):
                        ins = mm(ps[:, b, WCOLS:2 * WCOLS], pT[:, k, P * i:P * (i + 1)],
                                 w_proj[:, k, WCOLS * m:WCOLS * (m + 1)], k == 0, k == KP - 1)
                    ins.then_inc(ple_mm, 1)
                meet(pe, layer)


_INS = ["x_prompt", "x_sample", "state_gla", "state_gdn", "state_conv", "p_prompt", "p_sample",
        "norm_mix", "w_in", "w_gla_up", "b_gla_gate", "gla_norm", "conv_w", "gdn_a_log",
        "gdn_dt_bias", "gdn_norm", "w_out", "norm_ffn", "w_peer_q", "peer_sub_keys", "peer_u",
        "peer_v", "norm_ple", "w_ple_gate", "b_ple_gate", "w_ple_proj", "norm_final"]


def _outs(i):
    shape = {k: tuple(v.shape) for k, v in i.items()}
    depth, batch = shape["state_gla"][0], shape["x_prompt"][0]
    out = [shape["x_prompt"], shape["x_sample"]]
    for n in (batch, None):
        for s in ("state_gla", "state_gdn", "state_conv"):
            rest = shape[s][2:]
            out.append((depth, n if n is not None else shape[s][1]) + rest)
    return out


def kernel(**inputs):
    import numpy as _np
    import concourse.bacc as _bacc
    from concourse import mybir as _mybir
    from concourse.bass_utils import run_bass_kernel_spmd as _run

    nc = _bacc.Bacc("TRN2", target_bir_lowering=False, num_devices=1)
    arrays, args = {}, []
    for name in _INS:
        a = _np.ascontiguousarray(inputs[name])
        arrays[f"in_{name}_dram"] = a
        args.append(nc.dram_tensor(f"in_{name}_dram", a.shape, _mybir.dt.from_np(a.dtype),
                                   kind="ExternalInput").ap())
    shapes = _outs(inputs)
    for i, shape in enumerate(shapes):
        args.append(nc.dram_tensor(f"out_{i}_dram", shape, _mybir.dt.float32,
                                   kind="ExternalOutput").ap())
    hybrid_trunk(nc, *args)
    r = _run(nc, [arrays], core_ids=[0])
    return tuple(r.results[0][f"out_{i}_dram"] for i in range(len(shapes)))
```

```python
from contextlib import ExitStack

import concourse.bass as bass
from concourse import mybir

F32 = mybir.dt.float32
U32 = mybir.dt.uint32
ALU = mybir.AluOpType
ACT = mybir.ActivationFunctionType
AX = mybir.AxisListType.X

P = 128
EPS = 1e-6
GATE_NORM = 16.0
LOWEST = -3.0e38
TILES = 3
CONV_W = 4
GLA_CHUNK = 64
SUB = 16
TOPK = 16
G = 8
WCOLS = 256
RING = 4
BANK = 512


def hybrid_trunk(nc, x_prompt, x_sample, state_gla, state_gdn, state_conv, p_prompt, p_sample,
                 norm_mix, w_in, w_gla_up, b_gla_gate, gla_norm, conv_w, gdn_a_log, gdn_dt_bias,
                 gdn_norm, w_out, norm_ffn, w_peer_q, peer_sub_keys, peer_u, peer_v, norm_ple,
                 w_ple_gate, b_ple_gate, w_ple_proj, norm_final,
                 y_prompt, y_sample, gla_p, gdn_p, conv_p, gla_s, gdn_s, conv_s):
    DEPTH, NB, HG, DK, DV = state_gla.shape
    HD = state_gdn.shape[2]
    SEQ, D = x_prompt.shape[1:]
    TS = x_sample.shape[1]
    NSAMP = NB * TS
    NT = SEQ + NSAMP
    KD = D // P
    NEXP = peer_u.shape[1]
    HP, NK = peer_sub_keys.shape[1], peer_sub_keys.shape[3]
    PLE = p_prompt.shape[3]
    KP = PLE // P
    QD = HG * DK
    VD = HG * DV
    RANK = w_gla_up.shape[1]
    C_V1 = 2 * QD
    C_R1 = C_V1 + VD
    C_LR = C_R1 + VD
    C_QKV = C_LR + RANK
    C_Z = C_QKV + 3 * VD
    C_BA = C_Z + VD
    NQK, NC3, NH = 2 * QD // P, 3 * VD // P, 4
    ROWS = [P, P, NSAMP]
    COL = [0, P, 2 * P]
    STEPS = [HP, HP, HP // 2]
    NSTEP = sum(STEPS)
    assert SEQ == 2 * P and NSAMP == 64 and DV == P and DK == 64 and NT == 320

    blocks = [(w_in, c) for c in (0, 256, C_V1, C_V1 + 256, C_R1, C_R1 + 256)]
    blocks += [(w_in, C_QKV + WCOLS * n) for n in range(2 * 4)]
    blocks += [(w_out, WCOLS * n) for n in range(D // WCOLS)]
    blocks += [(w_peer_q, WCOLS * n) for n in range(w_peer_q.shape[2] // WCOLS)]
    blocks += [(w_ple_gate, WCOLS * n) for n in range(D // WCOLS)]
    B_OUT, B_PQ = 14, 14 + D // WCOLS
    B_PLE = B_PQ + w_peer_q.shape[2] // WCOLS

    ctx = ExitStack()
    with ctx:
        def sb(name, shape, dt=F32):
            return ctx.enter_context(nc.sbuf_tensor(name, shape, dt))

        h = sb("h", [P, TILES, D])
        xn = sb("xn", [P, TILES, D])
        aT = sb("aT", [P, KD, TILES * P])
        wring = sb("wring", [P, RING, KD, WCOLS])
        par_rows = sb("par_rows", [P, P])
        par = sb("par", [P, 76])
        PAR_MIX, PAR_FFN, PAR_PLE, PAR_CONV, PAR_GLA, PAR_GDN, PAR_BG = 0, 8, 16, 24, 72, 73, 74
        gain_row = sb("gain_row", [P, D])
        bias_row = sb("bias_row", [1, D])
        pT = sb("pT", [P, KP, TILES * P])
        ident = sb("ident", [P, P])
        twin = sb("twin", [P, P])
        ones = sb("ones", [P, P])
        zero = sb("zero", [P, P])
        incl64 = sb("incl64", [P, P])
        incl128 = sb("incl128", [P, P])
        low128 = sb("low128", [P, P])
        sub16 = sb("sub16", [P, P])
        incl8 = sb("incl8", [64, 64])
        low8 = sb("low8", [64, 64])
        same8 = sb("same8", [64, 64])
        seqmask = sb("seqmask", [64, NB])
        half_of = sb("half_of", [P, 2])
        reset = sb("reset", [P, NT])
        iota16 = sb("iota16", [P, TOPK])
        ssq = sb("ssq", [P, 4])
        rstd = sb("rstd", [P, 4])
        eps = sb("eps", [P, 1])
        ad = sb("ad", [P, 2, HD])
        ba = sb("ba", [P, TILES, 2 * HD])
        beta = sb("beta", [P, TILES, HD])
        soft = sb("soft", [P, TILES, HD])
        ypos = sb("ypos", [P, TILES, HD])
        g_tok = sb("g_tok", [P, TILES, HD])
        gst = sb("gst", [P, TILES, 2 * HD])
        eb = sb("eb", [P, TILES, 2 * HD])
        kds = sb("kds", [P, TILES, HD])
        idx_u = sb("idx_u", [P, 2, TOPK], U32)
        gate = sb("gate", [P, 2, TOPK])
        hid = sb("hid", [P, 2, TOPK])
        gelu = sb("gelu", [P, 2, TOPK])
        wgt = sb("wgt", [P, 2, TOPK])
        top = sb("top", [P, 2, TOPK])
        topi = sb("topi", [P, 2, TOPK], U32)
        topf = sb("topf", [P, 2, TOPK])
        cv = sb("cv", [P, TOPK])
        ci = sb("ci", [P, TOPK], U32)
        cij = sb("cij", [P, 2, TOPK], U32)
        cijf = sb("cijf", [P, 2, TOPK])
        pick = sb("pick", [P, 2, TOPK])
        idx_f = sb("idx_f", [P, TOPK])
        ncv = sb("ncv", [P, 2])
        esum = sb("esum", [P, 2])
        gexp = sb("gexp", [P, TOPK])
        table_base = sb("table_base", [P, 1])

        ARENA = 29216
        arena = sb("arena", [P, ARENA])

        def view(off, *dims, rows=P):
            n = 1
            for d in dims:
                n *= d
            assert off + n <= ARENA, (off, dims)
            v = arena[0:rows, off:off + n]
            if len(dims) == 2:
                v = v.rearrange("p (a b) -> p a b", b=dims[1])
            elif len(dims) == 3:
                v = v.rearrange("p (a b c) -> p a b c", b=dims[1], c=dims[2])
            return v

        zs = view(0, NH, NT)
        qkvc = view(1280, NC3, NT)
        halo = view(5120, NC3, NB * (CONV_W - 1 + TS))
        raw = view(6176, NC3, NT)
        ptok = view(6176, TILES, PLE)
        k2tok = view(6176, TILES, VD)
        v2tok = view(8192, TILES, VD)
        kq_S = view(5120, 2, NH, 64)
        dS = view(10016, NH, P)
        dSs = view(10528, NB, NH, P)
        vmask = view(14624, NH, NB, P, rows=64)
        l2sq = view(5632, 2 * NH * NT)
        conv_rows = view(18720, NC3 * P, rows=27)
        hist_rows = view(18720, NC3 * P, rows=24)
        lrT = view(20256, NT, rows=RANK)
        w_lrba = view(20576, KD, 24)
        tail = view(20256, NC3, 27)
        w_up = view(20768, QD, rows=RANK)
        Z = 21024
        q1k1 = view(Z, NQK, NT)
        gS = view(Z + 1280, 2, P)
        gSs = view(Z + 1536, NB * 2, P)
        gb = view(Z + 3584, 2, NT)
        q_mid = view(Z + 4224, 2, NT)
        k_mid = view(Z + 4864, 2, NT)
        k_last = view(Z + 5504, 2, NT)
        e_all = view(Z + 6144, 2, NT)
        q_all = view(Z + 6784, 2, NT)
        k_tok = view(Z + 7424, TILES, QD)
        attT = aT[:, 4:8, :].rearrange("p a b -> p (a b)")
        xflat = xn[:, :, :].rearrange("p a b -> p (a b)")
        v1 = xflat[:, 0:TILES * VD].rearrange("p (a b) -> p a b", b=VD)
        rs = xflat[:, TILES * VD:TILES * VD + NH * NT].rearrange("p (a b) -> p a b", b=NT)

        def slot(n, rows=P):
            flat = view(Z + 512 * n, 512) if n < 16 else xflat[:, 512 * (n - 16):512 * (n - 15)]
            return flat[0:rows, :].rearrange("p (a b) -> p a b", b=P)

        SA, SB, SC, SD, SF = [0, 7, 14], [1, 8, 15], [2, 9, 16], [3, 10, 17], [4, 11, 18]
        SO, SH, SQK = [5, 12], [6, 13], [19, 20, 21]

        def temp(i, which, rows=P):
            return view(14624 + 1024 * i + 512 * which, NH, P, rows=rows)

        def vnew(i, rows=P):
            return view(18720 + 512 * i, NH, P, rows=rows)

        k_one = view(6176, 2, 2 * NT)
        q_one = aT[:, 0:4, :].rearrange("p a b -> p (a b)")[:, 0:4 * NT].rearrange(
            "p (a b) -> p a b", a=2)
        kd = k2tok
        exp_b = qkvc[:, 2 * NH:3 * NH, :]
        dvm = [view(Z + 512 * (0, 2, 7, 9)[hd], NB, P, rows=64) for hd in range(NH)]

        def squares(which, i):
            off = Z + 4224 + 512 * i if which == 0 else Z + 512 * (14 + i)
            if which == 1 and i == 2:
                return xflat[:, 0:NH * ROWS[2]]
            return view(off, NH * ROWS[i])

        ORDER = [(0, 1, 2), (0, 2, 1)]
        SUM_BANK = [(6, 7, 6), (7, 7, 6)]
        MIX_BANK = (3, 7, 6, 5)
        XT_BANK = [(2, 4), (0, 1), (2, 4)]
        OUT_ORDER = ORDER[1]
        oall = aT

        urow = view(0, G, D)
        vrow = view(G * D, G, D)
        keys_n = view(0, 2 * HP, P)
        qT = view(26112, 2, TILES * P)
        scores = view(16384, NSTEP, 2, NK)
        keysT = view(21504, 2 * HP, NK)
        diag = view(23552, G, P)
        onehot = view(24576, 2, TOPK, TOPK)
        cand = view(25088, TOPK, TOPK)
        cand2 = view(25344, TOPK * TOPK)
        s_cur = view(25600, 2, NK)
        s_cut = view(25856, 2, NK)
        w_proj = view(26880, KP, D)
        sig = view(26112, 2, WCOLS)
        AHEAD = 2
        behind = {HP: [(0, None)], 2 * HP: [(1, None)],
                  2 * HP + 1: [(1, 0), (1, 1)], 2 * HP + 2: [(1, 2), (1, 3)]}
        for m_ in range(4):
            behind[HP + 1 + m_] = [(0, m_)]
        behind[NSTEP - 1] = [(2, None)] + [(2, m_) for m_ in range(4)]

        ps = ctx.enter_context(nc.psum_tensor("ps", [P, 8, BANK], F32))

        def bank(n, rows=P, cols=BANK):
            return ps[0:rows, n, 0:cols]

        def heads(n, rows=P, cols=P):
            return ps[0:rows, n, 0:NH * P].rearrange("p (a b) -> p a b", b=P)[:, :, 0:cols]

        def sem(name):
            return ctx.enter_context(nc.semaphore(name))

        x_loaded, const_ready, layer_done, cleared = map(
            sem, ("x_loaded", "const_ready", "layer_done", "cleared"))
        y_stored = sem("y_stored")
        pool_made, met = map(sem, ("pool_made", "met"))
        layer_sems = []

        def lsem(name):
            layer_sems.append(sem(name))
            return layer_sems[-1]

        par_loaded = lsem("par_loaded")
        ptok_loaded = lsem("ptok_loaded")
        small_loaded = lsem("small_loaded")
        hist_loaded = lsem("hist_loaded")
        gSs_loaded = lsem("gSs_loaded")
        dSs_loaded = lsem("dSs_loaded")
        rows_loaded = lsem("rows_loaded")
        keys_loaded = lsem("keys_loaded")
        wproj_loaded = lsem("wproj_loaded")
        w_loaded = [lsem(f"w_loaded{r}") for r in range(RING)]
        block_used = lsem("block_used")
        first_T = lsem("first_T")
        par_ready = lsem("par_ready")
        pT_ready = lsem("pT_ready")
        hist_ready = lsem("hist_ready")
        sq_done = lsem("sq_done")
        var_ready = lsem("var_ready")
        std_ready = lsem("std_ready")
        xn_ready = lsem("xn_ready")
        xT_done = lsem("xT_done")
        aT_ready = lsem("aT_ready")
        unit_mm = lsem("unit_mm")
        unit_out = lsem("unit_out")
        y_in = lsem("y_in")
        soft_ready = lsem("soft_ready")
        g_ready = lsem("g_ready")
        gate_mm = lsem("gate_mm")
        gx_ready = lsem("gx_ready")
        gl_args = lsem("gl_args")
        gl_exps = lsem("gl_exps")
        gl_ops = lsem("gl_ops")
        one_ready = lsem("one_ready")
        kd_T = lsem("kd_T")
        k_tok_ready = lsem("k_tok_ready")
        att_mm = lsem("att_mm")
        att_ready = lsem("att_ready")
        gU_mm = lsem("gU_mm")
        gS_ready = lsem("gS_ready")
        go_mm = lsem("go_mm")
        gvm_ready = lsem("gvm_ready")
        gs_decayed = lsem("gs_decayed")
        gs_mm = lsem("gs_mm")
        gs_add = lsem("gs_add")
        on_sq = lsem("on_sq")
        on_sum = lsem("on_sum")
        on_ln = lsem("on_ln")
        on_inv = lsem("on_inv")
        o_ready = lsem("o_ready")
        conv_done = lsem("conv_done")
        qkv_act = lsem("qkv_act")
        tail_ready = lsem("tail_ready")
        conv_rows_ready = lsem("conv_rows_ready")
        l2_sq = lsem("l2_sq")
        l2_sum = lsem("l2_sum")
        l2_ln = lsem("l2_ln")
        l2_inv = lsem("l2_inv")
        qk_ready = lsem("qk_ready")
        k2_T = lsem("k2_T")
        k2tok_ready = lsem("k2tok_ready")
        v2_T = lsem("v2_T")
        v2tok_ready = lsem("v2tok_ready")
        gst_mm = lsem("gst_mm")
        gst_ready = lsem("gst_ready")
        gst_exp = lsem("gst_exp")
        kd_ready = lsem("kd_ready")
        bB_mm = lsem("bB_mm")
        G_mm = lsem("G_mm")
        dargs = lsem("dargs")
        dexp = lsem("dexp")
        P1_ready = lsem("P1_ready")
        P1T_mm = lsem("P1T_mm")
        P1T_out = lsem("P1T_out")
        F0_ready = lsem("F0_ready")
        qk_mm = lsem("qk_mm")
        qkT_ready = lsem("qkT_ready")
        qd_ready = lsem("qd_ready")
        solve_mm = lsem("solve_mm")
        solve_act = lsem("solve_act")
        solve_dve = lsem("solve_dve")
        kS_mm = lsem("kS_mm")
        kq_mm = lsem("kq_mm")
        kq_out = lsem("kq_out")
        kST_T = lsem("kST_T")
        rs_ready = lsem("rs_ready")
        vs_mm = lsem("vs_mm")
        vs_ready = lsem("vs_ready")
        r_ready = lsem("r_ready")
        y_mm = lsem("y_mm")
        y_out = lsem("y_out")
        vn_mm = lsem("vn_mm")
        vn_ready = lsem("vn_ready")
        do_mm = lsem("do_mm")
        dU_mm = lsem("dU_mm")
        dS_ready = lsem("dS_ready")
        dvm_ready = lsem("dvm_ready")
        ds_decayed = lsem("ds_decayed")
        ds_mm = lsem("ds_mm")
        ds_add = lsem("ds_add")
        stored = [lsem(f"stored_{n}") for n in ("gla_p", "gla_s", "conv_p", "conv_s", "gdn_p", "gdn_s")]
        mix_mm = lsem("mix_mm")
        mix_add = lsem("mix_add")
        q_mm = lsem("q_mm")
        q_out = lsem("q_out")
        key_T = lsem("key_T")
        key_out = lsem("key_out")
        score_mm = lsem("score_mm")
        score_out = lsem("score_out")
        cv_ready = lsem("cv_ready")
        gate_exp = lsem("gate_exp")
        idx_ready = lsem("idx_ready")
        u_loaded = [lsem(f"u_loaded{r}") for r in range(G)]
        v_loaded = [lsem(f"v_loaded{r}") for r in range(G)]
        u_free = lsem("u_free")
        v_free = lsem("v_free")
        gathers = lsem("gathers")
        gelu_ready = lsem("gelu_ready")
        wgt_ready = lsem("wgt_ready")
        diag_ready = lsem("diag_ready")
        h_added = lsem("h_added")
        ple_mm = lsem("ple_mm")
        ple_sig = lsem("ple_sig")
        ple_done = lsem("ple_done")
        act_step = lsem("act_step")
        dve_step = lsem("dve_step")
        pick_step = sem("pick_step")
        first, last = layer_sems[0].num, layer_sems[-1].num
        assert last - first == len(layer_sems) - 1

        class Steps:

            def __init__(self, eng, own):
                self.eng, self.own, self.n = eng, own, 0

            def after(self, ins):
                self.n += 1
                ins.then_inc(self.own, 1)

            def settle(self):
                self.eng.wait_ge(self.own, self.n)

        def meet(eng, layer):
            eng.drain().then_inc(layer_done, 1)
            eng.wait_ge(cleared, layer + 1)

        def row(t, layer):
            return t[bass.ds(layer, 1), :]

        def of(t, layer):
            s = t[(bass.ds(layer, 1),) + (slice(None),) * (len(t.shape) - 1)]
            names = " ".join("abcdef"[:len(t.shape) - 1])
            first_, rest = names[0], names[2:]
            return s.rearrange(f"o {names} -> (o {first_}) {rest}")

        block = ctx.enter_context(nc.Block())
        xp = x_prompt.rearrange("o (i p) d -> p (o i) d", p=P)
        xs = x_sample.rearrange("b t d -> (b t) d")

        @block.sync
        def _(sp):
            sp.dma_start(h[:, 0:2, :], xp).then_inc(x_loaded, 16)
            sp.dma_start(h[0:64, 2, :], xs).then_inc(x_loaded, 16)
            sp.dma_start(h[64:P, 2, :], xs).then_inc(x_loaded, 16)
            with sp.Fori(0, DEPTH) as layer:
                for t, r0, n in ((norm_mix, PAR_MIX, KD), (norm_ffn, PAR_FFN, KD),
                                 (norm_ple, PAR_PLE, KD), (gla_norm, PAR_GLA, 1),
                                 (gdn_norm, PAR_GDN, 1), (b_gla_gate, PAR_BG, 2)):
                    sp.dma_start(par_rows[r0:r0 + n, :],
                                 row(t, layer).rearrange("o (k p) -> (o k) p", p=P)
                                 ).then_inc(par_loaded, 16)
                sp.dma_start(par_rows[PAR_CONV:PAR_CONV + CONV_W * NC3, :],
                             conv_w[bass.ds(layer, 1), :, :].rearrange("o j (k p) -> (o j k) p", p=P)
                             ).then_inc(par_loaded, 16)
                pp = p_prompt[bass.ds(layer, 1), 0, :, :].rearrange("o (i p) d -> p (o i) d", p=P)
                pz = p_sample[bass.ds(layer, 1), :, :, :].rearrange("o b t d -> (o b t) d")
                sp.dma_start(ptok[:, 0:2, :], pp).then_inc(ptok_loaded, 16)
                sp.dma_start(ptok[0:64, 2, :], pz).then_inc(ptok_loaded, 16)
                sp.dma_start(ptok[64:P, 2, :], pz).then_inc(ptok_loaded, 16)
                w_l = w_in[bass.ds(layer, 1), :, :]
                sp.dma_start(w_lrba[:, :, 0:RANK],
                             w_l[:, :, C_LR:C_LR + RANK].rearrange("o (k p) n -> p (o k) n", p=P)
                             ).then_inc(small_loaded, 16)
                sp.dma_start(w_lrba[:, :, RANK:24],
                             w_l[:, :, C_BA:C_BA + 2 * HD].rearrange("o (k p) n -> p (o k) n", p=P)
                             ).then_inc(small_loaded, 16)
                sp.dma_start(w_up[:, :], of(w_gla_up, layer)).then_inc(small_loaded, 16)
                sp.dma_start(ad[:, 0, :], row(gdn_a_log, layer).to_broadcast([P, HD])
                             ).then_inc(small_loaded, 16)
                sp.dma_start(ad[:, 1, :], row(gdn_dt_bias, layer).to_broadcast([P, HD])
                             ).then_inc(small_loaded, 16)
                sp.dma_start(hist_rows[:, :], state_conv[bass.ds(layer, 1), :, :, :].rearrange(
                    "o b j c -> (o b j) c")).then_inc(hist_loaded, 16)

                def load_block(n):
                    t, c = blocks[n]
                    if n >= RING:
                        sp.wait_ge(block_used, n - RING + 1)
                    sp.dma_start(wring[:, n % RING, :, :],
                                 t[bass.ds(layer, 1), :, c:c + WCOLS].rearrange(
                                     "o (k p) n -> p (o k) n", p=P)).then_inc(w_loaded[n % RING], 16)

                for n in range(RING):
                    load_block(n)
                sp.dma_start(gain_row[:, :], row(norm_ffn, layer).to_broadcast([P, D])
                             ).then_inc(rows_loaded, 16)
                sp.dma_start(bias_row[:, :], row(b_ple_gate, layer)).then_inc(rows_loaded, 16)
                for n in range(RING, B_PQ + RING):
                    load_block(n)
                sp.wait_ge(mix_add, 12)
                for n in range(B_PQ + RING, len(blocks)):
                    load_block(n)
                sp.dma_start(w_proj[:, :, :], w_ple_proj[bass.ds(layer, 1), :, :].rearrange(
                    "o (k p) n -> p (o k) n", p=P)).then_inc(wproj_loaded, 16)
                sp.drain().then_inc(layer_done, 1)
                sp.wait_ge(layer_done, (layer + 1) * 5)
                sp.sem_inc(met, 1)
                sp.sem_clear(range(first, last + 1))
                sp.drain().then_inc(cleared, 1)
            sp.dma_start(gain_row[:, :], norm_final.rearrange("(o d) -> o d", o=1).to_broadcast([P, D])
                         ).then_inc(rows_loaded, 16)
            sp.wait_ge(xn_ready, 3)
            sp.dma_start(y_prompt.rearrange("o (i p) d -> p (o i) d", p=P), xn[:, 0:2, :]
                         ).then_inc(y_stored, 16)
            sp.dma_start(y_sample.rearrange("b t d -> (b t) d"), xn[0:64, 2, :]
                         ).then_inc(y_stored, 16)
            sp.wait_ge(y_stored, 32)

        @block.gpsimd
        def _(pool):
            made = Steps(pool, pool_made)
            for t, value in ((ident, 0.0), (twin, 0.0), (ones, 1.0), (zero, 0.0), (incl64, 1.0),
                             (incl128, 1.0), (low128, 1.0), (sub16, 1.0), (incl8, 1.0), (low8, 1.0),
                             (same8, 1.0), (seqmask, 1.0), (half_of, 1.0), (reset, 1.0), (ba, 0.0), (gst, 0.0),
                             (eps, EPS), (table_base, 0.0), (hid, 0.0)):
                made.after(pool.memset(t[:], value))
            made.after(pool.iota(iota16[:, :], pattern=[[1, TOPK]], base=0, channel_multiplier=0,
                                 allow_small_or_imprecise_dtypes=True))
            made.settle()

            def select(t, pattern, base, mult, op=ALU.is_ge, fill=0.0):
                made.after(pool.affine_select(out=t, in_=t, compare_op=op, fill=fill, base=base,
                                              pattern=pattern, channel_multiplier=mult))
                made.settle()

            def same_block(t, nb, size):
                v = t[:, :].rearrange("p (b j) -> p b j", j=size)
                select(v, [[-size, nb], [0, size]], 0, 1)
                select(v, [[size, nb], [0, size]], size - 1, -1)

            select(ident[:, :], [[-1, P]], 0, 1, ALU.not_equal, 1.0)
            for off in (0, 64, -64):
                select(twin[:, :], [[-1, P]], off, 1, ALU.not_equal, 1.0)
            same_block(incl64, 2, GLA_CHUNK)
            same_block(sub16, P // SUB, SUB)
            for t in (incl8, low8, same8):
                same_block(t, NB, TS)
            for t, n in ((incl64, P), (incl128, P), (incl8, 64)):
                select(t[:, :], [[1, n]], 0, -1)
            for t, n in ((low128, P), (low8, 64)):
                select(t[:, :], [[-1, n]], -1, 1)
            select(seqmask[:, :], [[-TS, NB]], 0, 1)
            select(half_of[:, 0:1], [[0, 1]], 63, -1)
            select(half_of[:, 1:2], [[0, 1]], -64, 1)
            select(seqmask[:, :], [[TS, NB]], TS - 1, -1)
            for v, n in ((reset[:, 0:SEQ].rearrange("p (c t) -> p c t", t=GLA_CHUNK), GLA_CHUNK),
                         (reset[:, SEQ:NT].rearrange("p (c t) -> p c t", t=TS), TS)):
                select(v, [[0, v.shape[1]], [1, n]], -1, 0)
            pool.sem_inc(const_ready, 1)

            with pool.Fori(0, DEPTH) as layer:
                pool.wait_ge(xT_done, 1)
                pool.dma_start(gSs[:, :, :], state_gla[bass.ds(layer, 1), :, :, :, :].rearrange(
                    "o b (r s) k v -> (s k) (o b r) v", s=2)).then_inc(gSs_loaded, 16)
                pool.dma_start(dSs.rearrange("p b g v -> p (b g) v"),
                             state_gdn[bass.ds(layer, 1), :, :, :, :].rearrange(
                                 "o b g k v -> k (o b g) v")).then_inc(dSs_loaded, 16)
                pool.wait_ge(unit_out, 12)
                for hd in range(NH):
                    ins = pool.tensor_tensor(
                        vmask[:, hd, :, :],
                        v1[0:64, 2, hd * P:(hd + 1) * P].unsqueeze(1).to_broadcast([64, NB, P]),
                        seqmask[:, :].unsqueeze(2).to_broadcast([64, NB, P]), ALU.mult)
                ins.then_inc(gvm_ready, 1)
                pool.wait_ge(go_mm, 3)
                for r in range(2):
                    d = e_all[:, r, SEQ:NT].rearrange("p (b t) -> p b t", t=TS)[:, :, TS - 1:TS]
                    s_ = gSs[:, :, :].rearrange("p (b r) v -> p b r v", r=2)[:, :, r, :]
                    ins = pool.tensor_tensor(s_, s_, d.to_broadcast([P, NB, P]), ALU.mult)
                ins.then_inc(gs_decayed, 1)
                pool.wait_ge(gS_ready, 4)
                pool.dma_start(gla_p[bass.ds(layer, 1), 0, :, :, :].rearrange(
                    "o (r s) k v -> (s k) (o r) v", s=2), gS[:, :, :]).then_inc(stored[0], 16)
                pool.wait_ge(gs_add, 8)
                pool.dma_start(gla_s[bass.ds(layer, 1), :, :, :, :].rearrange(
                    "o b (r s) k v -> (s k) (o b r) v", s=2), gSs[:, :, :]
                ).then_inc(stored[1], 16)
                pool.wait_ge(conv_rows_ready, 1)
                pool.dma_start(conv_p[bass.ds(layer, 1), 0, :, :].rearrange("o j c -> (o j) c"),
                               conv_rows[0:3, :]).then_inc(stored[2], 16)
                pool.dma_start(conv_s[bass.ds(layer, 1), :, :, :].rearrange("o b j c -> (o b j) c"),
                               conv_rows[3:27, :]).then_inc(stored[3], 16)
                pool.wait_ge(k2tok_ready, 3)
                pool.wait_ge(gst_exp, 1)
                for i in range(TILES):
                    R = ROWS[i]
                    ins = pool.tensor_tensor(
                        kd[0:R, i, :].rearrange("p (a b) -> p a b", b=P),
                        k2tok[0:R, i, :].rearrange("p (a b) -> p a b", b=P),
                        kds[0:R, i, :].unsqueeze(2).to_broadcast([R, NH, P]), ALU.mult)
                ins.then_inc(kd_ready, 1)
                pool.wait_ge(dexp, 3)
                pool.wait_ge(qk_mm, 3)
                pool.wait_ge(kq_out, 1)
                pool.tensor_tensor(qkvc[:, 0:NH, :], qkvc[:, 0:NH, :], exp_b[:, :, :], ALU.mult)
                pool.tensor_tensor(kq_S[:, 0, :, :], kq_S[:, 0, :, :], exp_b[:, :, SEQ:NT],
                                   ALU.mult).then_inc(qd_ready, 1)
                for hd in range(NH):
                    d = exp_b[:, hd, SEQ:NT].rearrange("p (b t) -> p b t", t=TS)[:, :, TS - 1:TS]
                    ins = pool.tensor_tensor(dSs[:, :, hd, :], dSs[:, :, hd, :],
                                             d.to_broadcast([P, NB, P]), ALU.mult)
                ins.then_inc(ds_decayed, 1)
                pool.wait_ge(vs_ready, 1)
                for hd in range(NH):
                    ins = pool.tensor_tensor(
                        dvm[hd],
                        vnew(2, 64)[:, hd, :].unsqueeze(1).to_broadcast([64, NB, P]),
                        seqmask[:, :].unsqueeze(2).to_broadcast([64, NB, P]), ALU.mult)
                ins.then_inc(dvm_ready, 1)
                pool.wait_ge(dS_ready, 2)
                pool.dma_start(gdn_p[bass.ds(layer, 1), 0, :, :, :].rearrange(
                    "o g k v -> k (o g) v"), dS[:, :, :]).then_inc(stored[4], 16)
                pool.wait_ge(o_ready, 6)
                pool.dma_start(keys_n[:, :, :], peer_sub_keys[bass.ds(layer, 1), :, :, :, :].rearrange(
                    "o g c n d -> n (o g c) d")).then_inc(keys_loaded, 16)
                pool.wait_ge(ds_add, 8)
                pool.dma_start(gdn_s[bass.ds(layer, 1), :, :, :, :].rearrange(
                    "o b g k v -> k (o b g) v"), dSs.rearrange("p b g v -> p (b g) v")
                ).then_inc(stored[5], 16)
                for done in stored:
                    pool.wait_ge(done, 16)
                pool.wait_ge(key_T, 4)
                u_l = peer_u.rearrange("l e d -> (l e) d")
                v_l = peer_v.rearrange("l e d -> (l e) d")

                def gather_pair(pair):
                    for par_ in range(2):
                        step = pair * 2 + par_
                        pool.wait_ge(idx_ready, step + 1)
                        for half in range(2):
                            done = step * TOPK + half * G
                            for r in range(G):
                                at = idx_u[:, par_, half * G + r:half * G + r + 1]
                                pool.wait_ge(u_free, done + r + 1)
                                pool.sem_inc(gathers, 1)
                                pool.indirect_dma_start(
                                    urow[:, r, :], None, u_l,
                                    bass.IndirectOffsetOnAxis(ap=at, axis=0)).then_inc(u_loaded[r], 16)
                            for r in range(G):
                                at = idx_u[:, par_, half * G + r:half * G + r + 1]
                                pool.wait_ge(v_free, done + r + 1)
                                pool.sem_inc(gathers, 1)
                                pool.indirect_dma_start(
                                    vrow[:, r, :], None, v_l,
                                    bass.IndirectOffsetOnAxis(ap=at, axis=0)).then_inc(v_loaded[r], 16)

                with pool.Fori(0, NSTEP // 2) as pair:
                    gather_pair(pair)
                pool.wait_ge(u_free, G + NSTEP * TOPK)
                pool.wait_ge(v_free, G + NSTEP * TOPK)
                pool.dma_reset(range(first, last + 1))
                meet(pool, layer)

        units = [("lr", 0, None), ("ba", 0, None)]
        units += [("q1k1", f, f // 2) for f in range(NQK)]
        units += [("v1", (m, i), 2 + m) for m in range(2) for i in range(TILES)]
        units += [("r1", f, 4 + f // 2) for f in range(NH)]
        units += [("qkv", f, 6 + f // 2) for f in range(NC3)]
        units += [("z", f, 12 + f // 2) for f in range(NH)]
        U_QKV = 16

        solve = [(SC, SB, SA, "act"), (SD, SA, SB, "dve"), (SF, SC, SF, "+"),
                 (SA, SD, SC, "act"), (SB, SC, SD, "dve"), (SF, SA, SF, "+"),
                 (SC, SB, SA, "act"), (SF, SC, SF, "+"),
                 (SA, SF, SO, "act"), (SB, SO, SF, "dve"), (SC, SB, SA, "act"),
                 (SD, SA, SB, "dve"), (SH, SC, SH, "+"), (SA, SD, SC, "act"), (SH, SA, SH, "+")]
        INNER, N_T = 6, 9

        def solve_tiles(k):
            return (0, 1, 2) if k < INNER else (0, 1)

        def evacuations(upto, who):
            return sum(len(solve_tiles(k)) for k in range(upto) if (solve[k][3] == "act") == (who == "act"))

        @block.scalar
        def _(act):
            def norm(own):
                for i in range(TILES):
                    act.activation(xn[:, i, :], h[:, i, :], ACT.Square,
                                   accum_out=ssq[:, i:i + 1]).then_inc(sq_done, 1)
                act.wait_ge(var_ready, 1)
                act.activation(rstd[:, 0:3], ssq[:, 0:3], ACT.Sqrt).then_inc(std_ready, 1)
                act.wait_ge(par_ready, 1)
                for k in range(KD):
                    act.wait_ge(xT_done, k + 1)
                    g0 = PAR_MIX + k
                    act.activation(aT[:, k, :], ps[:, k % 2, 0:TILES * P], ACT.Copy,
                                   scale=par[:, g0:g0 + 1]).then_inc(aT_ready, 1)

            def out_square(which, n):
                i = ORDER[which][n]
                R = ROWS[i]
                act.wait_ge(go_mm if which == 0 else do_mm, n + 1)
                if which == 0:
                    act.wait_ge(att_ready, 3)
                act.activation(squares(which, i).rearrange("p (a b) -> p a b", b=R),
                               heads(3 + i, P, R), ACT.Square).then_inc(on_sq, 1)

            def out_log(which, n):
                i = ORDER[which][n]
                act.wait_ge(on_sum, TILES * which + n + 1)
                act.activation(squares(which, i), bank(SUM_BANK[which][n], cols=NH * ROWS[i]), ACT.Ln,
                               bias=eps[:, 0:1], scale=1.0 / P).then_inc(on_ln, 1)

            def out_inverse(which, n):
                act.wait_ge(on_ln, TILES * which + n + 1)
                v = squares(which, ORDER[which][n])
                act.activation(v, v, ACT.Exp, scale=-0.5).then_inc(on_inv, 1)

            def out_norm(which):
                for n in range(TILES):
                    out_square(which, n)
                for n in range(TILES):
                    out_log(which, n)
                for n in range(TILES):
                    out_inverse(which, n)

            act.wait_ge(const_ready, 1)
            act.wait_ge(x_loaded, 48)
            with act.Fori(0, DEPTH) as layer:
                own = Steps(act, act_step)
                norm(own)
                act.wait_ge(first_T, 2)
                act.activation(pT[:, 0, :], ps[:, 5, 0:TILES * P], ACT.Copy)
                act.activation(pT[:, 1, :], ps[:, 6, 0:TILES * P], ACT.Copy).then_inc(pT_ready, 1)

                def conv_silu(f):
                    act.wait_ge(conv_done, f + 1)
                    act.activation(qkvc[:, f, :], qkvc[:, f, :], ACT.Silu).then_inc(qkv_act, 1)

                for n, (name, f, blk) in enumerate(units):
                    b = 2 + n % 4
                    act.wait_ge(unit_mm, n + 1)
                    if name == "lr":
                        ins = act.activation(lrT[:, :], ps[0:RANK, b, 0:NT], ACT.Copy)
                    elif name == "ba":
                        act.activation(ba[:, 0:2, :], ps[:, b, 0:16].rearrange(
                            "p (i n) -> p i n", n=8), ACT.Copy)
                        ins = act.activation(ba[0:64, 2, :], ps[0:64, b, 16:24], ACT.Copy)
                    elif name == "q1k1":
                        ins = act.activation(q1k1[:, f, :], ps[:, b, 0:NT], ACT.Copy)
                    elif name == "v1":
                        m, i = f
                        R = ROWS[i]
                        ins = act.activation(v1[0:R, i, WCOLS * m:WCOLS * (m + 1)],
                                             ps[0:R, b, 0:WCOLS], ACT.Copy)
                    elif name == "r1":
                        ins = act.activation(rs[:, f, :], ps[:, b, 0:NT], ACT.Silu)
                    elif name == "z":
                        ins = act.activation(zs[:, f, :], ps[:, b, 0:NT], ACT.Silu)
                    else:
                        if f == 0:
                            act.wait_ge(hist_ready, 1)
                        act.activation(raw[:, f, 0:SEQ], ps[:, b, 0:SEQ], ACT.Copy)
                        ins = act.activation(
                            halo[:, f, :].rearrange("p (b t) -> p b t", b=NB)[:, :, CONV_W - 1:],
                            ps[:, b, SEQ:NT].rearrange("p (b t) -> p b t", b=NB), ACT.Copy)
                    ins.then_inc(unit_out, 1)
                    if name == "qkv" and f >= 2:
                        conv_silu(f - 2)
                    if n == 5:
                        act.wait_ge(gate_mm, 1)
                        for r in range(2):
                            own.after(act.activation(gb[:, r, :], ps[:, 6 + r, 0:NT], ACT.Identity,
                                                     bias=par[:, PAR_BG + r:PAR_BG + r + 1]))
                        act.wait_ge(y_in, 1)
                        own.after(act.activation(soft[:, :, :], ypos[:, :, :], ACT.Abs))
                        own.settle()
                        own.after(act.activation(q_mid[:, :, :], gb[:, :, :], ACT.Abs))
                        own.settle()
                        own.after(act.activation(soft[:, :, :], soft[:, :, :], ACT.Exp, scale=-1.0))
                        own.after(act.activation(q_mid[:, :, :], q_mid[:, :, :], ACT.Exp, scale=-1.0))
                        own.after(act.activation(ad[:, 0, :], ad[:, 0, :], ACT.Exp))
                        own.settle()
                        act.activation(soft[:, :, :], soft[:, :, :], ACT.Ln, bias=ones[:, 0:1])
                        act.activation(q_mid[:, :, :], q_mid[:, :, :], ACT.Ln,
                                       bias=ones[:, 0:1]).then_inc(gx_ready, 1)
                        act.activation(beta[:, :, :], ba[:, :, 0:HD], ACT.Sigmoid
                                       ).then_inc(soft_ready, 1)
                    if n == 14:
                        act.wait_ge(gst_ready, 1)
                        act.activation(eb[:, :, :], gst[:, :, :], ACT.Exp)
                        act.activation(kds[:, :, :], kds[:, :, :], ACT.Exp).then_inc(gst_exp, 1)
                    if n == 11:
                        act.wait_ge(gl_args, 1)
                        s = 1.0 / GATE_NORM
                        own.after(act.activation(k_mid[:, :, :], q_mid[:, :, :], ACT.Exp, scale=-s))
                        own.settle()
                        act.activation(q_mid[:, :, :], q_mid[:, :, :], ACT.Exp, scale=s)
                        act.activation(k_last[:, :, :], k_last[:, :, :], ACT.Exp, scale=-s)
                        act.activation(e_all[:, :, :], gb[:, :, :], ACT.Exp, scale=s
                                       ).then_inc(gl_exps, 1)
                conv_silu(NC3 - 2)
                conv_silu(NC3 - 1)

                act.wait_ge(kd_T, 1)
                act.activation(k_tok[:, 0:2, :].rearrange("p a b -> p (a b)"), bank(6), ACT.Copy)
                act.activation(k_tok[0:64, 2, :], ps[0:64, 7, 0:QD], ACT.Copy
                               ).then_inc(k_tok_ready, 1)
                act.wait_ge(qkv_act, NC3)
                act.wait_ge(tail_ready, 1)
                act.wait_ge(att_mm, 3)
                for m in range(5):
                    c = slice(512 * m, 512 * (m + 1))
                    act.activation(l2sq[:, c], qkvc[:, 0:2 * NH, :].rearrange("p a b -> p (a b)")[:, c],
                                   ACT.Square).then_inc(l2_sq, 1)
                for m in range(5):
                    act.wait_ge(l2_sum, m + 1)
                    act.activation(l2sq[:, 512 * m:512 * (m + 1)], bank(m % 3), ACT.Ln,
                                   bias=eps[:, 0:1]).then_inc(l2_ln, 1)
                act.wait_ge(l2_ln, 5)
                for s_ in range(2):
                    v = l2sq[:, NH * NT * s_:NH * NT * (s_ + 1)]
                    act.activation(v, v, ACT.Exp, scale=-0.5).then_inc(l2_inv, 1)
                out_norm(0)
                for i in range(TILES):
                    act.wait_ge(v2_T, i + 1)
                    act.activation(v2tok[0:ROWS[i], i, :], bank(i, ROWS[i]), ACT.Copy
                                   ).then_inc(v2tok_ready, 1)
                for i in range(TILES):
                    act.wait_ge(k2_T, i + 1)
                    act.activation(k2tok[0:ROWS[i], i, :], bank(i, ROWS[i]), ACT.Copy
                                   ).then_inc(k2tok_ready, 1)
                act.wait_ge(first_T, 4)
                for b in range(3):
                    ins = act.activation(conv_rows[:, 512 * b:512 * (b + 1)], bank(3 + b, 27), ACT.Copy)
                ins.then_inc(conv_rows_ready, 1)
                for i in range(TILES):
                    R = ROWS[i]
                    act.wait_ge(dargs, i + 1)
                    act.activation(temp(i, 0, R)[:, :, 0:R], temp(i, 0, R)[:, :, 0:R], ACT.Exp,
                                   scale=-1.0)
                    act.activation(temp(i, 1, R)[:, :, 0:R], temp(i, 1, R)[:, :, 0:R], ACT.Exp)
                    act.wait_ge(v2_T, 3)
                    act.activation(exp_b[:, :, COL[i]:COL[i] + R], heads(i, P, R), ACT.Exp
                                   ).then_inc(dexp, 1)
                act.wait_ge(kq_mm, 1)
                act.activation(kq_S[:, :, :, :].rearrange("p w h t -> p (w h t)"), bank(7), ACT.Copy
                               ).then_inc(kq_out, 1)
                for i in range(TILES):
                    R = ROWS[i]
                    act.wait_ge(P1T_mm, i + 1)
                    act.activation(slot(SB[i], R)[:, :, 0:R], heads(3 + i, R, R), ACT.Copy
                                   ).then_inc(P1T_out, 1)
                n = 0
                for k, (to, _, _, who) in enumerate(solve):
                    for i in solve_tiles(k):
                        n += 1
                        if who == "act":
                            R = ROWS[i]
                            act.wait_ge(solve_mm, n)
                            act.activation(slot(to[i], R)[:, :, 0:R], heads(i + 3 * (k % 2), R, R),
                                           ACT.Copy).then_inc(solve_act, 1)
                for i in range(2):
                    act.wait_ge(y_mm, i + 1)
                    act.activation(temp(i, 0), heads(1), ACT.Copy).then_inc(y_out, 1)
                    if i == 0:
                        for done in stored[2:4]:
                            act.wait_ge(done, 16)
                        act.wait_ge(vs_mm, 1)
                        act.activation(vnew(2, 64), heads(7, 64), ACT.Copy).then_inc(vs_ready, 1)
                    else:
                        out_log(1, 1)
                    act.wait_ge(vn_mm, i + 1)
                    act.activation(vnew(i), heads(2), ACT.Copy).then_inc(vn_ready, 1)
                    if i == 0:
                        out_square(1, 0)
                        out_square(1, 1)
                        out_log(1, 0)
                out_inverse(1, 0)
                out_inverse(1, 1)
                out_square(1, 2)
                out_log(1, 2)
                out_inverse(1, 2)

                def softmax(step):
                    act.wait_ge(cv_ready, step + 1)
                    act.activation(gexp[:, :], cv[:, :], ACT.Exp, bias=ncv[:, 0:1],
                                   accum_out=esum[:, 0:1]).then_inc(gate_exp, 1)

                def first_scores():
                    act.wait_ge(q_mm, 1)
                    act.activation(qT[:, :, 0:P], bank(4, cols=2 * P).rearrange(
                        "p (c t) -> p c t", c=2), ACT.Copy).then_inc(q_out, 1)
                    act.wait_ge(score_mm, 1)
                    act.activation(scores[:, 0:1, :, :].rearrange("p a b c -> p (a b c)"),
                                   ps[:, 4, 2 * P:2 * P + 2 * NK], ACT.Copy).then_inc(score_out, 1)

                for n, i in enumerate(OUT_ORDER):
                    act.wait_ge(mix_add, 4 * (n + 1))
                    act.activation(xn[:, i, :], h[:, i, :], ACT.Square,
                                   accum_out=ssq[:, i:i + 1]).then_inc(sq_done, 1)
                    act.wait_ge(var_ready, n + 2)
                    act.activation(rstd[:, i:i + 1], ssq[:, i:i + 1], ACT.Sqrt
                                   ).then_inc(std_ready, 1)
                    if n == 1:
                        first_scores()
                    act.wait_ge(xT_done, KD + n + 1)
                    for b in range(2):
                        ins = act.activation(aT[:, 4 * b:4 * b + 4, P * i:P * (i + 1)],
                                             heads(XT_BANK[n][b]), ACT.Copy)
                    ins.then_inc(aT_ready, 1)
                    if n == 1:
                        softmax(0)

                def queries(hd):
                    t0 = P if hd == 0 else 0
                    for c in range(2):
                        act.wait_ge(q_mm, 1 + 2 * hd + c + 1)
                        act.activation(qT[:, c, t0:NT], ps[:, 6 + c, t0:NT], ACT.Copy)
                        act.activation(qT[:, c, NT:], ps[:, 6 + c, SEQ:NT], ACT.Copy
                                       ).then_inc(q_out, 1)

                def score(hd):
                    flat = "p a b c -> p (a b c)"
                    act.wait_ge(score_mm, hd + 2)
                    for i in range(1 if hd == 0 else 0, 2):
                        act.activation(scores[:, HP * i + hd:HP * i + hd + 1, :, :].rearrange(flat),
                                       ps[:, 6, 2 * NK * i:2 * NK * (i + 1)], ACT.Copy)
                    rows, s0 = slice(64 * (hd // 4), 64 * (hd // 4) + 64), 2 * HP + hd % 4
                    act.activation(scores[rows, s0:s0 + 1, :, :].rearrange(flat),
                                   ps[rows, 7, 0:2 * NK], ACT.Copy).then_inc(score_out, 1)

                for hd in range(AHEAD):
                    queries(hd)
                    score(hd)

                def weights(step, par_, half, unit):
                    c = slice(half * G, half * G + G)
                    done = step * TOPK + half * G
                    act.wait_ge(u_free, done + 2 * G)
                    act.activation(gelu[:, par_, c], hid[:, par_, c], ACT.Gelu
                                   ).then_inc(gelu_ready, 1)
                    act.wait_ge(wgt_ready, step * 2 + half + 1)
                    for r in range(G):
                        act.wait_ge(v_free, done + r + 1)
                        k = half * G + r
                        act.activation(diag[:, r, :], unit[:, :], ACT.Copy,
                                       scale=wgt[:, par_, k:k + 1]).then_inc(diag_ready, 1)

                def embed(i, m):
                    if m is None:
                        act.wait_ge(h_added, i + 1)
                        act.activation(xn[:, i, :], h[:, i, :], ACT.Square,
                                       accum_out=ssq[:, i:i + 1]).then_inc(sq_done, 1)
                        act.wait_ge(var_ready, 4 + i + 1)
                        act.activation(rstd[:, i:i + 1], ssq[:, i:i + 1], ACT.Sqrt
                                       ).then_inc(std_ready, 1)
                        act.wait_ge(xT_done, KD + 3 + i + 1)
                        for k in range(KD):
                            g0 = PAR_PLE + k
                            ins = act.activation(
                                aT[:, k, P * i:P * (i + 1)],
                                ps[:, 6 + k // 4, P * (k % 4):P * (k % 4 + 1)], ACT.Copy,
                                scale=par[:, g0:g0 + 1])
                        ins.then_inc(aT_ready, 1)
                        return
                    n = 4 * i + m
                    act.wait_ge(ple_mm, n + 1)
                    if n >= 2:
                        act.wait_ge(ple_done, n - 1)
                    act.activation(sig[:, n % 2, :], ps[:, 6 + n % 2, 0:WCOLS], ACT.Sigmoid
                                   ).then_inc(ple_sig, 1)

                for step in range(NSTEP):
                    unit = ident if step < 2 * HP else twin
                    weights(step, step % 2, 0, unit)
                    if step < NSTEP - 1:
                        softmax(step + 1)
                    if step + AHEAD < HP:
                        queries(step + AHEAD)
                    weights(step, step % 2, 1, unit)
                    if step + AHEAD < HP:
                        score(step + AHEAD)
                    for i, m in behind.get(step, ()):
                        embed(i, m)
                meet(act, layer)
            for i in range(TILES):
                act.activation(xn[:, i, :], h[:, i, :], ACT.Square,
                               accum_out=ssq[:, i:i + 1]).then_inc(sq_done, 1)
            act.wait_ge(var_ready, 1)
            act.activation(rstd[:, 0:3], ssq[:, 0:3], ACT.Sqrt).then_inc(std_ready, 1)

        @block.vector
        def _(dve):
            def norm(own):
                dve.wait_ge(sq_done, TILES)
                dve.tensor_scalar(ssq[:, 0:3], ssq[:, 0:3], 1.0 / D, EPS, ALU.mult, ALU.add
                                  ).then_inc(var_ready, 1)
                dve.wait_ge(std_ready, 1)
                own.after(dve.reciprocal(rstd[:, 0:3], rstd[:, 0:3]))
                own.settle()
                for i in range(TILES):
                    dve.tensor_scalar(xn[:, i, :], h[:, i, :], rstd[:, i:i + 1], None, ALU.mult
                                      ).then_inc(xn_ready, 1)

            def tile_rstd(i, before, own):
                dve.wait_ge(sq_done, before + 3)
                dve.tensor_scalar(ssq[:, i:i + 1], ssq[:, i:i + 1], 1.0 / D, EPS, ALU.mult,
                                  ALU.add).then_inc(var_ready, 1)
                dve.wait_ge(std_ready, before + 1)
                own.after(dve.reciprocal(rstd[:, i:i + 1], rstd[:, i:i + 1]))
                own.settle()

            def over_heads(t, R):
                return t[0:R, 0:R].unsqueeze(1).to_broadcast([R, NH, R])

            def per_head(t, R, n=P):
                return t.unsqueeze(2).to_broadcast([R, NH, n])

            def out_norm(which, own):
                gain = par[:, PAR_GLA + which:PAR_GLA + which + 1]
                for n, i in enumerate(ORDER[which]):
                    R = ROWS[i]
                    v3 = squares(which, i).rearrange("p (a b) -> p a b", b=R)
                    dve.wait_ge(on_inv, TILES * which + n + 1)
                    own.after(dve.tensor_tensor(v3, v3, heads(3 + i, P, R), ALU.mult))
                    own.settle()
                    silu = (rs if which == 0 else zs)[:, :, COL[i]:COL[i] + R]
                    o4 = oall[:, 4 * which:4 * which + 4, :]
                    ins = dve.scalar_tensor_tensor(o4[:, :, COL[i]:COL[i] + R], v3, gain, silu,
                                                   ALU.mult, ALU.mult)
                    if i == 2:
                        ins = dve.scalar_tensor_tensor(o4[:, :, NT:NT + R], v3, gain, silu,
                                                       ALU.mult, ALU.mult)
                    ins.then_inc(o_ready, 1)

            def pick_experts(step, par_):
                own = Steps(dve, pick_step)
                own.after(dve.tensor_copy(s_cur[:, :, :], scores[:, step, :, :]))
                own.settle()
                for c in range(2):
                    own.after(dve.max(top[:, c, 0:8], s_cur[:, c, :]))
                own.settle()
                for c in range(2):
                    own.after(dve.match_replace(s_cut[:, c, :], top[:, c, 0:8], s_cur[:, c, :],
                                                LOWEST))
                    own.after(dve.max_index(topi[:, c, 0:8], top[:, c, 0:8], s_cur[:, c, :]))
                own.settle()
                for c in range(2):
                    own.after(dve.max(top[:, c, 8:16], s_cut[:, c, :]))
                own.settle()
                own.after(dve.tensor_tensor(
                    cand[:, :, :], top[:, 0, :].unsqueeze(2).to_broadcast([P, TOPK, TOPK]),
                    top[:, 1, :].unsqueeze(1).to_broadcast([P, TOPK, TOPK]), ALU.add))
                for c in range(2):
                    own.after(dve.max_index(topi[:, c, 8:16], top[:, c, 8:16], s_cut[:, c, :]))
                own.settle()
                cf = cand[:, :, :].rearrange("p a b -> p (a b)")
                own.after(dve.tensor_copy(topf[:, :, :], topi[:, :, :]))
                own.after(dve.max(cv[:, 0:8], cf))
                own.settle()
                own.after(dve.match_replace(cand2[:, :], cv[:, 0:8], cf, LOWEST))
                own.after(dve.max_index(ci[:, 0:8], cv[:, 0:8], cf))
                own.after(dve.tensor_scalar(ncv[:, 0:1], cv[:, 0:1], -1.0, None, ALU.mult))
                own.settle()
                own.after(dve.max(cv[:, 8:16], cand2[:, :]))
                own.settle()
                dve.max_index(ci[:, 8:16], cv[:, 8:16], cand2[:, :]).then_inc(cv_ready, 1)
                dve.wait_ge(cv_ready, step + 1)
                own.after(dve.tensor_scalar(cij[:, 0, :], ci[:, :], 4, None,
                                            ALU.logical_shift_right))
                own.after(dve.tensor_scalar(cij[:, 1, :], ci[:, :], 15, None, ALU.bitwise_and))
                own.settle()
                own.after(dve.tensor_copy(cijf[:, :, :], cij[:, :, :]))
                own.settle()
                own.after(dve.tensor_tensor(
                    onehot[:, :, :, :].rearrange("p c k n -> p (c k) n"),
                    iota16[:, :].unsqueeze(1).to_broadcast([P, 2 * TOPK, TOPK]),
                    cijf[:, :, :].rearrange("p c k -> p (c k)").unsqueeze(2)
                    .to_broadcast([P, 2 * TOPK, TOPK]), ALU.is_equal))
                own.settle()
                own.after(dve.tensor_tensor(
                    onehot[:, :, :, :], onehot[:, :, :, :],
                    topf[:, :, :].unsqueeze(2).to_broadcast([P, 2, TOPK, TOPK]), ALU.mult))
                own.settle()
                own.after(dve.tensor_reduce(pick[:, :, :], onehot[:, :, :, :], AX, ALU.add))
                own.settle()
                own.after(dve.scalar_tensor_tensor(idx_f[:, :], pick[:, 0, :], float(NK),
                                                   pick[:, 1, :], ALU.mult, ALU.add))
                dve.wait_ge(gate_exp, step + 1)
                own.after(dve.reciprocal(esum[:, 1:2], esum[:, 0:1]))
                own.settle()
                dve.tensor_scalar(gate[:, par_, :], gexp[:, :], esum[:, 1:2], None, ALU.mult)
                if step > 0:
                    dve.wait_ge(v_free, step * TOPK - TOPK + G)
                dve.tensor_scalar(idx_u[:, par_, :], idx_f[:, :], table_base[:, 0:1], None,
                                  ALU.add).then_inc(idx_ready, 1)
                dve.sem_clear(pick_step)

            def dots(step, par_, half, tile):
                for r in range(G):
                    dve.wait_ge(u_loaded[r], (step * 2 + half + 1) * 16)
                    k = half * G + r
                    dve.tensor_tensor_reduce(
                        out=urow[:, r, :], in0=urow[:, r, :], in1=xn[:, tile, :], scale=1.0,
                        scalar=0.0, op0=ALU.mult, op1=ALU.add,
                        accum_out=hid[:, par_, k:k + 1]).then_inc(u_free, 1)
                dve.wait_ge(gelu_ready, step * 2 + half + 1)
                c = slice(half * G, half * G + G)
                dve.tensor_tensor(wgt[:, par_, c], gelu[:, par_, c], gate[:, par_, c], ALU.mult
                                  ).then_inc(wgt_ready, 1)

            def embed(i, m, own):
                if m is None:
                    dve.wait_ge(v_free, G + TOPK * sum(STEPS[:i + 1]))
                    dve.tensor_tensor(h[:, i, :], h[:, i, :],
                                      ps[:, 2 * i:2 * i + 2, :].rearrange("p a b -> p (a b)"),
                                      ALU.add).then_inc(h_added, 1)
                    tile_rstd(i, TILES + i + 1, own)
                    dve.tensor_scalar(xn[:, i, :], h[:, i, :], rstd[:, i:i + 1], None, ALU.mult
                                      ).then_inc(xn_ready, 1)
                    return
                n = 4 * i + m
                t, g_ = h[:, i, WCOLS * m:WCOLS * (m + 1)], sig[:, n % 2, :]
                dve.wait_ge(ple_sig, n + 1)
                own.after(dve.tensor_tensor(g_, g_, ps[:, 6 + n % 2, WCOLS:2 * WCOLS], ALU.mult))
                own.settle()
                dve.tensor_tensor(t, t, g_, ALU.add).then_inc(ple_done, 1)

            dve.wait_ge(const_ready, 1)
            with dve.Fori(0, DEPTH) as layer:
                own = Steps(dve, dve_step)
                dve.wait_ge(first_T, 1)
                dve.tensor_copy(par[:, :], ps[:, 7, 0:76]).then_inc(par_ready, 1)
                norm(own)
                dve.wait_ge(first_T, 3)
                hv = halo[:, :, :].rearrange("p f (b t) -> p f b t", b=NB)
                for f in range(NC3):
                    ins = dve.tensor_copy(hv[:, f, :, 0:CONV_W - 1], ps[:, 4, 24 * f:24 * (f + 1)]
                                          .rearrange("p (b j) -> p b j", b=NB))
                ins.then_inc(hist_ready, 1)
                dve.wait_ge(small_loaded, 80)
                dve.wait_ge(unit_out, 2)
                own.after(dve.tensor_tensor(ypos[:, :, :], ba[:, :, HD:2 * HD],
                                            ad[:, 1, :].unsqueeze(1).to_broadcast([P, TILES, HD]),
                                            ALU.add))
                own.settle()
                dve.sem_inc(y_in, 1)
                dve.wait_ge(gx_ready, 1)
                own.after(dve.scalar_tensor_tensor(gb[:, :, :], gb[:, :, :], 0.0, q_mid[:, :, :],
                                                   ALU.min, ALU.subtract))
                own.settle()
                for r in range(2):
                    own.after(dve.tensor_tensor_scan(gb[:, r, :], reset[:, :], gb[:, r, :], 0.0,
                                                     ALU.mult, ALU.add))
                own.settle()
                for c0, c1, size in ((0, SEQ, GLA_CHUNK), (SEQ, NT, TS)):
                    n, mid = (c1 - c0) // size, size // 2 - 1
                    for r in range(2):
                        b3 = gb[:, r, c0:c1].rearrange("p (c t) -> p c t", t=size)
                        for to, at in ((q_mid, mid), (k_last, size - 1)):
                            ins = dve.tensor_tensor(
                                to[:, r, c0:c1].rearrange("p (c t) -> p c t", t=size), b3,
                                b3[:, :, at:at + 1].to_broadcast([P, n, size]), ALU.subtract)
                ins.then_inc(gl_args, 1)
                dve.wait_ge(soft_ready, 1)
                own.after(dve.scalar_tensor_tensor(soft[:, :, :], ypos[:, :, :], 0.0, soft[:, :, :],
                                                   ALU.max, ALU.add))
                own.settle()
                own.after(dve.tensor_scalar(soft[:, :, :], soft[:, :, :], -1.0, None, ALU.mult))
                own.settle()
                dve.tensor_tensor(g_tok[:, :, :], soft[:, :, :],
                                  ad[:, 0, :].unsqueeze(1).to_broadcast([P, TILES, HD]), ALU.mult
                                  ).then_inc(g_ready, 1)
                dve.wait_ge(gl_exps, 1)
                q1, k1 = q1k1[:, 0:2, :], q1k1[:, 2:4, :]
                scale = float(DK) ** -0.5
                dve.tensor_tensor(k_mid[:, :, :], k_mid[:, :, :], k1, ALU.mult)
                dve.tensor_tensor(k_last[:, :, :], k_last[:, :, :], k1, ALU.mult)
                dve.scalar_tensor_tensor(q_all[:, :, :], q1, scale, e_all[:, :, :], ALU.mult,
                                         ALU.mult)
                dve.scalar_tensor_tensor(q_mid[:, :, :], q1, scale, q_mid[:, :, :], ALU.mult,
                                         ALU.mult).then_inc(gl_ops, 1)
                dve.wait_ge(gst_mm, 1)
                dve.tensor_copy(gst[:, 0:2, :], ps[:, 6, 0:16].rearrange("p (i n) -> p i n", n=8))
                own.after(dve.tensor_copy(gst[0:64, 2, :], ps[0:64, 6, 16:24]))
                own.settle()
                dve.tensor_tensor(kds[:, :, :], gst[:, :, HD:2 * HD], gst[:, :, 0:HD], ALU.subtract
                                  ).then_inc(gst_ready, 1)
                for f in range(NC3):
                    dve.wait_ge(unit_out, U_QKV + f + 1)
                    hf = hv[:, f, :, :]
                    out_p = qkvc[:, f, 0:SEQ]
                    out_s = qkvc[:, f, SEQ:NT].rearrange("p (b t) -> p b t", t=TS)
                    for d in range(CONV_W):
                        j = CONV_W - 1 - d
                        w = par[:, PAR_CONV + NC3 * j + f:PAR_CONV + NC3 * j + f + 1]
                        if d == 0:
                            own.after(dve.tensor_scalar(out_p, raw[:, f, 0:SEQ], w, None, ALU.mult))
                            own.after(dve.tensor_scalar(out_s, hf[:, :, j:j + TS], w, None, ALU.mult))
                        else:
                            own.after(dve.scalar_tensor_tensor(
                                out_p[:, d:], raw[:, f, 0:SEQ - d], w, out_p[:, d:], ALU.mult,
                                ALU.add))
                            own.after(dve.scalar_tensor_tensor(
                                out_s, hf[:, :, j:j + TS], w, out_s, ALU.mult, ALU.add))
                        own.settle()
                    dve.sem_inc(conv_done, 1)
                dve.tensor_copy(tail[:, :, 3:27].rearrange("p f (b j) -> p f b j", b=NB),
                                hv[:, :, :, TS:TS + 3])
                dve.tensor_copy(tail[:, :, 0:3], raw[:, :, SEQ - 3:SEQ]).then_inc(tail_ready, 1)
                dve.wait_ge(tail_ready, 1)

                dve.wait_ge(unit_mm, len(units))
                flat = "p a b -> p (a b)"
                own.settle()
                for s_ in range(2):
                    dve.tensor_scalar(k_one[:, s_, :], k_mid[:, :, :].rearrange(flat),
                                      half_of[:, s_:s_ + 1], None, ALU.mult)
                    ins = dve.tensor_scalar(q_one[:, s_, :], q_all[:, :, :].rearrange(flat),
                                            half_of[:, s_:s_ + 1], None, ALU.mult)
                ins.then_inc(one_ready, 1)
                for i in range(TILES):
                    R = ROWS[i]
                    dve.wait_ge(att_mm, i + 1)
                    dve.tensor_tensor(
                        attT[0:R, 512 * i:512 * (i + 1)].rearrange("p (a b) -> p a b", b=P)[:, :, 0:R],
                        heads(i, R, R), over_heads(incl64 if i < 2 else incl8, R), ALU.mult
                    ).then_inc(att_ready, 1)
                for c in range(SEQ // GLA_CHUNK):
                    dve.wait_ge(gU_mm, c + 1)
                    at = GLA_CHUNK * (c + 1) - 1
                    for r in range(2):
                        for s_ in range(2):
                            rows = slice(64 * s_, 64 * s_ + 64)
                            u = ps[rows, 6 + c % 2, 256 * r + P * s_:256 * r + P * s_ + P]
                            if c == 0:
                                ins = dve.tensor_copy(gS[rows, r, :], u)
                            else:
                                ins = dve.scalar_tensor_tensor(
                                    gS[rows, r, :], gS[rows, r, :], e_all[rows, r, at:at + 1], u,
                                    ALU.mult, ALU.add)
                    ins.then_inc(gS_ready, 1)
                inv = l2sq[:, :].rearrange("p (a b) -> p a b", b=NT)
                dve.wait_ge(l2_inv, 1)
                dve.scalar_tensor_tensor(qkvc[:, 0:NH, :], qkvc[:, 0:NH, :], float(P) ** -0.5,
                                         inv[:, 0:NH, :], ALU.mult, ALU.mult)
                dve.wait_ge(l2_inv, 2)
                own.after(dve.tensor_tensor(qkvc[:, NH:2 * NH, :], qkvc[:, NH:2 * NH, :],
                                            inv[:, NH:2 * NH, :], ALU.mult))
                own.settle()
                dve.sem_inc(qk_ready, 1)
                dve.wait_ge(gs_decayed, 1)
                gs4 = gSs[:, :, :].rearrange("p (b r) v -> p b r v", r=2)
                for n in range(8):
                    hd, half = n // 2, n % 2
                    rows = slice(64 * (hd % 2), 64 * (hd % 2) + 64)
                    s_ = gs4[rows, 4 * half:4 * half + 4, hd // 2, :]
                    dve.wait_ge(gs_mm, n + 1)
                    dve.tensor_tensor(s_, s_, ps[rows, n % 3, :].rearrange("p (b v) -> p b v", b=4),
                                      ALU.add).then_inc(gs_add, 1)
                out_norm(0, own)
                for i in range(TILES):
                    R = ROWS[i]
                    dve.wait_ge(bB_mm, i + 1)
                    for hd in range(NH):
                        src, b_row = heads(i, R, R)[:, hd, :], gst[0:R, i, hd:hd + 1]
                        dve.tensor_scalar(temp(i, 0, R)[:, hd, 0:R], src, b_row, 0.0, ALU.subtract,
                                          ALU.max)
                        ins = dve.tensor_scalar(temp(i, 1, R)[:, hd, 0:R], src, b_row, 0.0,
                                                ALU.subtract, ALU.min)
                    ins.then_inc(dargs, 1)
                for done in stored[0:4]:
                    dve.wait_ge(done, 16)
                for i in range(TILES):
                    R = ROWS[i]
                    dec = temp(i, 0, R)[:, :, 0:R]
                    P1, low = slot(SA[i], R)[:, :, 0:R], (low128 if i < 2 else low8)
                    dve.wait_ge(dexp, i + 1)
                    for hd in range(NH):
                        own.after(dve.scalar_tensor_tensor(
                            dec[:, hd, :], dec[:, hd, :], beta[0:R, i, hd:hd + 1], low[0:R, 0:R],
                            ALU.mult, ALU.mult))
                    own.settle()
                    dve.wait_ge(G_mm, i + 1)
                    if i < 2:
                        own.after(dve.tensor_tensor(dec, heads(3 + i, R, R), dec, ALU.mult))
                        own.settle()
                        own.after(dve.tensor_tensor(P1, dec, over_heads(sub16, R), ALU.mult))
                        own.settle()
                        own.after(dve.tensor_tensor(slot(SO[i])[:, :, :], dec, P1, ALU.subtract))
                    else:
                        own.after(dve.tensor_tensor(P1, heads(3 + i, R, R), dec, ALU.mult))
                    own.settle()
                    dve.sem_inc(P1_ready, 1)
                for i in range(TILES):
                    R = ROWS[i]
                    d1 = temp(i, 1, R)[:, :, 0:R]
                    own.after(dve.tensor_tensor(d1, d1, over_heads(incl128 if i < 2 else incl8, R),
                                                ALU.mult))
                    own.settle()
                    dve.wait_ge(qk_mm, i + 1)
                    dve.tensor_tensor(slot(SQK[i], R)[:, :, 0:R], heads(i, R, R), d1, ALU.mult
                                      ).then_inc(qkT_ready, 1)
                for i in range(TILES):
                    R = ROWS[i]
                    dve.wait_ge(P1T_out, i + 1)
                    dve.scalar_tensor_tensor(slot(SF[i], R)[:, :, 0:R], slot(SB[i], R)[:, :, 0:R], -1.0,
                                             over_heads(ident, R), ALU.mult, ALU.add
                                             ).then_inc(F0_ready, 1)
                dve.wait_ge(qkT_ready, 3)
                dve.tensor_tensor(temp(0, 1), v2tok[:, 0, :].rearrange("p (a b) -> p a b", b=P),
                                  per_head(beta[:, 0, :], P), ALU.mult).then_inc(r_ready, 1)

                def r_of(i, k_S, done):
                    R = ROWS[i]
                    r_ = temp(i, 1, R)
                    own.after(dve.tensor_tensor(r_, k_S, per_head(eb[0:R, i, 0:HD], R), ALU.mult))
                    own.settle()
                    own.after(dve.tensor_tensor(r_, v2tok[0:R, i, :].rearrange("p (a b) -> p a b", b=P),
                                                r_, ALU.subtract))
                    own.settle()
                    dve.tensor_tensor(r_, r_, per_head(beta[0:R, i, :], R), ALU.mult
                                      ).then_inc(done, 1)

                dve.wait_ge(kST_T, 1)
                r_of(2, heads(7, 64), rs_ready)
                n = 0
                for k, (to, _, _, who) in enumerate(solve):
                    for i in solve_tiles(k):
                        n += 1
                        R = ROWS[i]
                        src, t = heads(i + 3 * (k % 2), R, R), slot(to[i], R)[:, :, 0:R]
                        if who == "act":
                            continue
                        dve.wait_ge(solve_mm, n)
                        if k == N_T:
                            own.after(dve.scalar_tensor_tensor(
                                slot(SH[i])[:, :, :], src, -1.0, over_heads(ident, R), ALU.mult,
                                ALU.add))
                        if who == "+":
                            dve.tensor_tensor(t, src, t, ALU.add).then_inc(solve_dve, 1)
                        else:
                            dve.tensor_copy(t, src).then_inc(solve_dve, 1)

                for i in range(2):
                    if i > 0:
                        dve.wait_ge(kS_mm, i)
                        r_of(i, heads(0), r_ready)
                    dve.wait_ge(dU_mm, i + 1)
                    for hd in range(NH):
                        u = heads(6)[:, hd, :]
                        if i == 0:
                            ins = dve.tensor_copy(dS[:, hd, :], u)
                        else:
                            ins = dve.scalar_tensor_tensor(
                                dS[:, hd, :], dS[:, hd, :], eb[:, i, HD + hd:HD + hd + 1], u,
                                ALU.mult, ALU.add)
                    ins.then_inc(dS_ready, 1)
                out_norm(1, own)

                dve.wait_ge(ds_decayed, 1)
                for n in range(12):
                    if n < 8:
                        hd, half = n // 2, n % 2
                        s_ = dSs[:, 4 * half:4 * half + 4, hd, :]
                        dve.wait_ge(ds_mm, n + 1)
                        dve.tensor_tensor(s_, s_, bank(n % 3).rearrange("p (b v) -> p b v", b=4),
                                          ALU.add).then_inc(ds_add, 1)
                    i, m = OUT_ORDER[n // 4], n % 4
                    t = h[:, i, WCOLS * m:WCOLS * (m + 1)]
                    dve.wait_ge(mix_mm, n + 1)
                    dve.tensor_tensor(t, t, bank(MIX_BANK[m], cols=WCOLS), ALU.add
                                      ).then_inc(mix_add, 1)
                    if m == 3:
                        tile_rstd(i, n // 4 + 1, own)
                        if n == 3:
                            dve.wait_ge(rows_loaded, 32)
                        dve.scalar_tensor_tensor(xn[:, i, :], h[:, i, :], rstd[:, i:i + 1],
                                                 gain_row[:, :], ALU.mult, ALU.mult
                                                 ).then_inc(xn_ready, 1)
                    if n in (7, 9):
                        for b in range(2):
                            at = (n - 7) + b
                            dve.wait_ge(key_T, at + 1)
                            dve.tensor_copy(keysT[:, 4 * at:4 * at + 4, :].rearrange(
                                "p a b -> p (a b)"), bank(b)).then_inc(key_out, 1)
                    if n == 10:
                        dve.sem_inc(u_free, G)
                        dve.wait_ge(score_out, 1)
                        pick_experts(0, 0)
                for step in range(NSTEP):
                    tile = step // HP
                    dots(step, step % 2, 0, tile)
                    if step + 1 < NSTEP:
                        dve.wait_ge(score_out, min(step + 3, HP + 1))
                        pick_experts(step + 1, (step + 1) % 2)
                    dots(step, step % 2, 1, tile)
                    for i, m in behind.get(step, ()):
                        embed(i, m, own)
                dve.tensor_scalar(table_base[:, :], table_base[:, :], float(NEXP), None, ALU.add)
                meet(dve, layer)
            dve.wait_ge(sq_done, 3)
            dve.tensor_scalar(ssq[:, 0:3], ssq[:, 0:3], 1.0 / D, EPS, ALU.mult, ALU.add
                              ).then_inc(var_ready, 1)
            dve.wait_ge(std_ready, 1)
            dve.wait_ge(rows_loaded, 16)
            dve.reciprocal(rstd[:, 0:3], rstd[:, 0:3]).then_inc(dve_step, 1)
            dve.wait_ge(dve_step, 1)
            for i in range(TILES):
                dve.scalar_tensor_tensor(xn[:, i, :], h[:, i, :], rstd[:, i:i + 1], gain_row[:, :],
                                         ALU.mult, ALU.mult).then_inc(xn_ready, 1)

        @block.tensor
        def _(pe):
            def mm(out, lhsT, rhs, start=True, stop=True):
                return pe.matmul(out, lhsT, rhs, start=start, stop=stop, skip_group_check=True)

            def transpose_rows():
                pe.wait_ge(xn_ready, TILES)
                for k in range(KD):
                    if k >= 2:
                        pe.wait_ge(aT_ready, k - 1)
                    for i in range(TILES):
                        ins = pe.transpose(ps[:, k % 2, P * i:P * (i + 1)],
                                           xn[:, i, P * k:P * (k + 1)], ident[:, :])
                    ins.then_inc(xT_done, 1)
                pe.wait_ge(aT_ready, KD)

            def transpose_tile(i, banks):
                for k in range(KD):
                    ins = pe.transpose(heads(banks[k // 4])[:, k % 4, :],
                                       xn[:, i, P * k:P * (k + 1)], ident[:, :])
                ins.then_inc(xT_done, 1)

            def arrived(n):
                pe.wait_ge(w_loaded[n % RING], 16 * (n // RING + 1))

            def product(out, n, c, cols, moving):
                for k in range(KD):
                    ins = mm(out, wring[:, n % RING, k, c:c + cols], moving(k), k == 0, k == KD - 1)
                return ins

            def out_sum(which, n):
                i = ORDER[which][n]
                pe.wait_ge(on_sq, TILES * which + n + 1)
                before = SUM_BANK[which][:n]
                if SUM_BANK[which][n] in before:
                    pe.wait_ge(on_ln, TILES * which + before.index(SUM_BANK[which][n]) + 1)
                mm(bank(SUM_BANK[which][n], cols=NH * ROWS[i]), ones[:, :], squares(which, i)
                   ).then_inc(on_sum, 1)

            pe.wait_ge(const_ready, 1)
            with pe.Fori(0, DEPTH) as layer:
                pe.wait_ge(par_loaded, 7 * 16)
                pe.transpose(ps[:, 7, 0:76], par_rows[0:76, :], ident[0:76, 0:76]).then_inc(first_T, 1)
                transpose_rows()
                pe.wait_ge(ptok_loaded, 48)
                for k in range(KP):
                    for i in range(TILES):
                        ins = pe.transpose(ps[:, 5 + k, P * i:P * (i + 1)],
                                           ptok[:, i, P * k:P * (k + 1)], ident[:, :])
                ins.then_inc(first_T, 1)
                pe.wait_ge(hist_loaded, 16)
                for f in range(NC3):
                    ins = pe.transpose(ps[:, 4, 24 * f:24 * (f + 1)], hist_rows[:, P * f:P * (f + 1)],
                                       ident[0:24, 0:24])
                ins.then_inc(first_T, 1)

                pe.wait_ge(small_loaded, 80)
                for n, (name, f, blk) in enumerate(units):
                    b = 2 + n % 4
                    if n >= 4:
                        pe.wait_ge(unit_out, n - 3)
                    if n == 2:
                        pe.wait_ge(hist_ready, 1)
                    if n == 3:
                        pe.wait_ge(pT_ready, 1)
                    if blk is not None:
                        arrived(blk)
                    tokens = lambda k: aT[:, k, 0:NT]
                    if name == "lr":
                        for k in range(KD):
                            ins = mm(ps[0:RANK, b, 0:NT], w_lrba[:, k, 0:RANK], tokens(k), k == 0,
                                     k == KD - 1)
                    elif name == "ba":
                        for i in range(TILES):
                            R = ROWS[i]
                            for k in range(KD):
                                ins = mm(ps[0:R, b, 8 * i:8 * i + 8], aT[:, k, COL[i]:COL[i] + R],
                                         w_lrba[:, k, RANK:24], k == 0, k == KD - 1)
                    elif name == "v1":
                        m, i = f
                        R = ROWS[i]
                        for k in range(KD):
                            ins = mm(ps[0:R, b, 0:WCOLS], aT[:, k, COL[i]:COL[i] + R],
                                     wring[:, blk % RING, k, :], k == 0, k == KD - 1)
                    else:
                        ins = product(ps[:, b, 0:NT], blk, P * (f % 2), P, tokens)
                    ins.then_inc(unit_mm, 1)
                    if blk is not None and (n + 1 == len(units) or units[n + 1][2] != blk):
                        pe.wait_ge(unit_mm, n + 1)
                        pe.sem_inc(block_used, 1)
                    if n == 13:
                        pe.wait_ge(g_ready, 1)
                        for i in range(TILES):
                            R = ROWS[i]
                            incl, same = (incl128, ones) if i < 2 else (incl8, same8)
                            mm(ps[0:R, 6, 8 * i:8 * i + 4], incl[0:R, 0:R], g_tok[0:R, i, :])
                            ins = mm(ps[0:R, 6, 8 * i + 4:8 * i + 8], same[0:R, 0:R],
                                     g_tok[0:R, i, :])
                        ins.then_inc(gst_mm, 1)
                    if n == 5:
                        pe.wait_ge(unit_out, 1)
                        for r in range(2):
                            ins = mm(ps[:, 6 + r, 0:NT], w_up[:, P * r:P * (r + 1)], lrT[:, :])
                        ins.then_inc(gate_mm, 1)

                pe.wait_ge(gl_ops, 1)
                for i in range(TILES):
                    R = ROWS[i]
                    for r in range(2):
                        c = 256 * (i % 2) + P * r
                        ins = pe.transpose(ps[0:R, 6 + i // 2, c:c + P],
                                           k_last[:, r, COL[i]:COL[i] + R], ident[:, :])
                ins.then_inc(kd_T, 1)

                def one(t, hd):
                    return t[:, hd % 2, NT * (hd // 2):NT * (hd // 2 + 1)]

                pe.wait_ge(one_ready, 1)
                pe.wait_ge(unit_out, len(units))
                for i in range(TILES):
                    R, c = ROWS[i], slice(COL[i], COL[i] + ROWS[i])
                    for hd in range(NH):
                        ins = mm(heads(i, R, R)[:, hd, :], one(k_one, hd)[:, c], q_mid[:, hd // 2, c])
                    ins.then_inc(att_mm, 1)
                for i in range(TILES):
                    R = ROWS[i]
                    pe.wait_ge(att_ready, i + 1)
                    for hd in range(NH):
                        mm(heads(3 + i, P, R)[:, hd, :], v1[0:R, i, P * hd:P * (hd + 1)],
                           attT[0:R, 512 * i + P * hd:512 * i + P * hd + R], hd == 0, False)
                def l2_sums(pieces):
                    for m in pieces:
                        pe.wait_ge(l2_sq, m + 1)
                        if m >= 3:
                            pe.wait_ge(l2_ln, m - 2)
                        mm(bank(m % 3), ones[:, :], l2sq[:, 512 * m:512 * (m + 1)]
                           ).then_inc(l2_sum, 1)

                def sample_outputs(sequences):
                    for b in sequences:
                        c = slice(SEQ + TS * b, SEQ + TS * (b + 1))
                        for hd in range(NH):
                            ins = mm(heads(5)[:, hd, TS * b:TS * (b + 1)], gSs[:, 2 * b + hd // 2, :],
                                     one(q_one, hd)[:, c], False, False)
                    return ins

                pe.wait_ge(k_tok_ready, 1)
                pe.wait_ge(gSs_loaded, 16)
                for c in range(SEQ // GLA_CHUNK):
                    i, s_ = c // 2, slice(64 * (c % 2), 64 * (c % 2) + 64)
                    if c > 0:
                        pe.wait_ge(gS_ready, c)
                        for hd in range(NH):
                            ins = mm(heads(3 + i)[:, hd, s_], gS[:, hd // 2, :],
                                     one(q_one, hd)[:, 64 * c:64 * c + 64], False, False)
                        if c % 2:
                            ins.then_inc(go_mm, 1)
                    for r in range(2):
                        ins = mm(ps[:, 6 + c % 2, 256 * r:256 * r + 256],
                                 k_tok[s_, i, P * r:P * (r + 1)], v1[s_, i, 256 * r:256 * r + 256])
                    ins.then_inc(gU_mm, 1)
                    if c == 0:
                        l2_sums(range(0, 3))
                    elif c == 1:
                        sample_outputs(range(0, 3))
                    elif c == 2:
                        l2_sums(range(3, 5))
                        sample_outputs(range(3, 5))
                    else:
                        sample_outputs(range(5, NB)).then_inc(go_mm, 1)
                pe.wait_ge(gvm_ready, 1)
                pe.wait_ge(l2_ln, 5)
                for n in range(8):
                    hd, half = n // 2, n % 2
                    if n >= 3:
                        pe.wait_ge(gs_add, n - 2)
                    if n == 3:
                        pe.wait_ge(gS_ready, 4)
                        for t_ in range(TILES):
                            out_sum(0, t_)
                    mm(bank(n % 3), k_tok[0:64, 2, P * (hd // 2):P * (hd // 2 + 1)],
                       vmask[:, hd, 4 * half:4 * half + 4, :]).then_inc(gs_mm, 1)
                pe.wait_ge(gs_add, 8)
                for i in range(TILES):
                    c = slice(COL[i], COL[i] + ROWS[i])
                    for hd in range(NH):
                        ins = pe.transpose(heads(i, ROWS[i])[:, hd, :], qkvc[:, 2 * NH + hd, c],
                                           ident[:, :])
                    ins.then_inc(v2_T, 1)
                pe.wait_ge(qk_ready, 1)
                for i in range(TILES):
                    c = slice(COL[i], COL[i] + ROWS[i])
                    pe.wait_ge(v2tok_ready, i + 1)
                    for hd in range(NH):
                        ins = pe.transpose(heads(i, ROWS[i])[:, hd, :], qkvc[:, NH + hd, c],
                                           ident[:, :])
                    ins.then_inc(k2_T, 1)
                pe.wait_ge(o_ready, 3)
                for f in range(NC3):
                    ins = pe.transpose(ps[0:27, 3 + f // 4, P * (f % 4):P * (f % 4 + 1)],
                                       tail[:, f, :], ident[:, :])
                ins.then_inc(first_T, 1)
                for i in range(TILES):
                    R = ROWS[i]
                    incl = incl128 if i < 2 else incl8
                    pe.wait_ge(k2tok_ready, i + 1)
                    for hd in range(NH):
                        ins = mm(heads(i, P, R)[:, hd, :],
                                 g_tok[0:R, i, hd:hd + 1].to_broadcast([R, P]), incl[0:R, 0:R])
                    ins.then_inc(bB_mm, 1)
                pe.wait_ge(conv_rows_ready, 1)
                for i in range(TILES):
                    R, c = ROWS[i], slice(COL[i], COL[i] + ROWS[i])
                    for hd in range(NH):
                        ins = mm(heads(3 + i, R, R)[:, hd, :], qkvc[:, NH + hd, c],
                                 qkvc[:, NH + hd, c])
                    ins.then_inc(G_mm, 1)
                for i in range(TILES):
                    R, c = ROWS[i], slice(COL[i], COL[i] + ROWS[i])
                    pe.wait_ge(dexp, i + 1)
                    for hd in range(NH):
                        ins = mm(heads(i, R, R)[:, hd, :], qkvc[:, NH + hd, c], qkvc[:, hd, c])
                    ins.then_inc(qk_mm, 1)
                pe.wait_ge(dSs_loaded, 16)
                pe.wait_ge(on_ln, 3)
                both = qkvc[:, 0:2 * NH, :].rearrange("p (w g) t -> p w g t", w=2)
                to = ps[:, 7, :].rearrange("p (w g t) -> p w g t", w=2, g=NH)
                for b in range(NB):
                    for hd in range(NH):
                        ins = mm(to[:, :, hd, TS * b:TS * (b + 1)], dSs[:, b, hd, :],
                                 both[:, :, hd, SEQ + TS * b:SEQ + TS * (b + 1)])
                ins.then_inc(kq_mm, 1)
                for i in range(TILES):
                    R = ROWS[i]
                    pe.wait_ge(P1_ready, i + 1)
                    for hd in range(NH):
                        ins = pe.transpose(heads(3 + i, R, R)[:, hd, :],
                                           slot(SA[i], R)[:, hd, 0:R], ident[0:R, 0:R])
                    ins.then_inc(P1T_mm, 1)
                pe.wait_ge(kq_out, 1)
                for hd in range(NH):
                    ins = pe.transpose(heads(7, 64)[:, hd, :], kq_S[:, 1, hd, :], ident[:, :])
                ins.then_inc(kST_T, 1)
                for k, (to, left, right, who) in enumerate(solve):
                    for i in solve_tiles(k):
                        R = ROWS[i]
                        if k == 0:
                            pe.wait_ge(P1T_out, i + 1)
                            pe.wait_ge(F0_ready, i + 1)
                            pe.wait_ge(qkT_ready, i + 1)
                        else:
                            by = solve[k - 1][3]
                            pe.wait_ge(solve_act if by == "act" else solve_dve,
                                       evacuations(k - 1, by) + i + 1)
                        for hd in range(NH):
                            ins = mm(heads(i + 3 * (k % 2), R, R)[:, hd, :],
                                     slot(left[i], R)[:, hd, 0:R], slot(right[i], R)[:, hd, 0:R])
                        ins.then_inc(solve_mm, 1)
                pe.wait_ge(solve_act, evacuations(len(solve), "act"))
                pe.wait_ge(solve_dve, evacuations(len(solve), "dve"))

                pe.wait_ge(kd_ready, 1)
                pe.wait_ge(qd_ready, 1)
                pe.wait_ge(rs_ready, 1)
                for i in range(2):
                    c = slice(COL[i], COL[i] + P)
                    if i == 1:
                        pe.wait_ge(dS_ready, 1)
                        for hd in range(NH):
                            ins = mm(heads(0)[:, hd, :], qkvc[:, NH + hd, c], dS[:, hd, :])
                        ins.then_inc(kS_mm, 1)
                        out_sum(1, 0)
                    pe.wait_ge(r_ready, i + 1)
                    for hd in range(NH):
                        ins = mm(heads(1)[:, hd, :], slot(SF[i])[:, hd, :], temp(i, 1)[:, hd, :])
                    ins.then_inc(y_mm, 1)
                    if i == 0:
                        for hd in range(NH):
                            ins = mm(heads(7, 64)[:, hd, :], slot(SF[2], 64)[:, hd, 0:64],
                                     temp(2, 1, 64)[:, hd, :])
                        ins.then_inc(vs_mm, 1)
                    else:
                        out_sum(1, 1)
                    pe.wait_ge(y_out, i + 1)
                    if i > 0:
                        pe.wait_ge(vn_ready, i)
                    for hd in range(NH):
                        ins = mm(heads(2)[:, hd, :], slot(SH[i])[:, hd, :], temp(i, 0)[:, hd, :])
                    ins.then_inc(vn_mm, 1)
                    if i == 1:
                        for hd in range(NH):
                            mm(heads(4)[:, hd, :], dS[:, hd, :], qkvc[:, hd, c], hd == 0, False)
                    pe.wait_ge(vn_ready, i + 1)

                    def state_products():
                        for hd in range(NH):
                            ins = mm(heads(6)[:, hd, :], kd[:, i, P * hd:P * (hd + 1)],
                                     vnew(i)[:, hd, :])
                        ins.then_inc(dU_mm, 1)

                    if i == 0:
                        state_products()
                    for hd in range(NH):
                        ins = mm(heads(3 + i)[:, hd, :], vnew(i)[:, hd, :],
                                 slot(SQK[i])[:, hd, :], i == 0 and hd == 0, False)
                    ins.then_inc(do_mm, 1)
                    if i == 1:
                        pe.wait_ge(dS_ready, 1)
                        state_products()
                    else:
                        pe.wait_ge(vs_ready, 1)
                        mm(heads(5, P, 64), ident[:, :], kq_S[:, 0, :, :], True, False)
                        for hd in range(NH):
                            ins = mm(heads(5, P, 64)[:, hd, :], vnew(2, 64)[:, hd, :],
                                     slot(SQK[2], 64)[:, hd, 0:64], False, False)
                        ins.then_inc(do_mm, 1)
                pe.wait_ge(dS_ready, 2)
                out_sum(1, 2)

                def sample_states(n):
                    hd, half = n // 2, n % 2
                    if n >= 3:
                        pe.wait_ge(ds_add, n - 2)
                    mm(bank(n % 3), kd[0:64, 2, P * hd:P * (hd + 1)],
                       dvm[hd][:, 4 * half:4 * half + 4, :]).then_inc(ds_mm, 1)

                pe.wait_ge(dvm_ready, 1)
                for n in range(3):
                    sample_states(n)
                for n in range(12):
                    i, m = OUT_ORDER[n // 4], n % 4
                    if m == 0:
                        pe.wait_ge(o_ready, 4 + n // 4)
                    if n < 4:
                        arrived(B_OUT + m)
                        if m == 1:
                            pe.wait_ge(on_ln, 5)
                        elif m == 2:
                            pe.wait_ge(on_ln, 6)
                        elif m == 3:
                            pe.wait_ge(o_ready, 5)
                    else:
                        pe.wait_ge(mix_add, n - 3)
                    for k in range(KD):
                        ins = mm(bank(MIX_BANK[m], cols=WCOLS), oall[:, k, P * i:P * (i + 1)],
                                 wring[:, (B_OUT + m) % RING, k, :], k == 0, k == KD - 1)
                    ins.then_inc(mix_mm, 1)
                    if n >= 8:
                        pe.wait_ge(mix_mm, n + 1)
                        pe.sem_inc(block_used, 1)
                    if n < 5:
                        sample_states(n + 3)
                    if n == 6:
                        pe.wait_ge(ds_add, 6)
                        pe.wait_ge(xn_ready, TILES + 1)
                        transpose_tile(OUT_ORDER[0], XT_BANK[0])
                    if n in (7, 9):
                        pe.wait_ge(ds_add, 8)
                        pe.wait_ge(keys_loaded, 16)
                        for b in range(2):
                            at = (n - 7) + b
                            if n == 9:
                                pe.wait_ge(key_out, b + 1)
                            for j in range(4):
                                ins = pe.transpose(heads(b)[:, j, :], keys_n[:, 4 * at + j, :],
                                                   ident[:, :])
                            ins.then_inc(key_T, 1)
                    if n == 9:
                        arrived(B_PQ)
                        pe.wait_ge(aT_ready, KD + 1)
                        for c in range(2):
                            ins = product(ps[:, 4, P * c:P * (c + 1)], B_PQ, P * c, P,
                                          lambda k: aT[:, k, 0:P])
                        ins.then_inc(q_mm, 1)
                    if n == 10:
                        pe.wait_ge(key_out, 4)
                        pe.wait_ge(q_out, 1)
                        for c in range(2):
                            ins = mm(ps[:, 4, P * (2 + c):P * (3 + c)], qT[:, c, 0:P],
                                     keysT[:, c, :])
                        ins.then_inc(score_mm, 1)
                        pe.wait_ge(xn_ready, TILES + 2)
                        transpose_tile(OUT_ORDER[1], XT_BANK[1])

                pe.sem_inc(v_free, G)
                pe.wait_ge(xn_ready, TILES + 3)
                pe.wait_ge(score_out, 1)
                transpose_tile(OUT_ORDER[2], XT_BANK[2])
                pe.wait_ge(aT_ready, KD + 3)

                def queries(hd):
                    blk, t0 = B_PQ + hd, P if hd == 0 else 0
                    arrived(blk)
                    pe.wait_ge(score_out, hd + 1)
                    for c in range(2):
                        product(ps[:, 6 + c, t0:NT], blk, P * c, P, lambda k: aT[:, k, t0:NT]
                                ).then_inc(q_mm, 1)
                    pe.wait_ge(q_mm, 1 + 2 * hd + 2)
                    pe.sem_inc(block_used, 1)

                def score(hd):
                    pe.wait_ge(q_out, 1 + 2 * hd + 2)
                    for i in range(1 if hd == 0 else 0, TILES):
                        for c in range(2):
                            ins = mm(ps[:, 6 + i // 2, 256 * (i % 2) + P * c:
                                        256 * (i % 2) + P * (c + 1)],
                                     qT[:, c, P * i:P * (i + 1)], keysT[:, 2 * hd + c, :])
                    ins.then_inc(score_mm, 1)

                queries(0)
                score(0)
                for b in range(6):
                    mm(bank(b), zero[:, :], zero[:, :].unsqueeze(1).to_broadcast([P, 4, P]))
                for hd in range(1, AHEAD):
                    queries(hd)
                    score(hd)

                def embed(i, m):
                    if m is None:
                        pe.wait_ge(xn_ready, 2 * TILES + i + 1)
                        if i > 0:
                            pe.wait_ge(ple_done, 4 * i)
                        else:
                            pe.wait_ge(score_out, HP + 1)
                        transpose_tile(i, (6, 7))
                        return
                    n, b, blk = 4 * i + m, 6 + (4 * i + m) % 2, B_PLE + m
                    if i == 0:
                        arrived(blk)
                    if m == 0:
                        pe.wait_ge(aT_ready, KD + 3 + i + 1)
                        pe.wait_ge(wproj_loaded, 16)
                    if n >= 2:
                        pe.wait_ge(ple_done, n - 1)
                    for k in range(KD):
                        mm(ps[:, b, 0:WCOLS], aT[:, k, P * i:P * (i + 1)],
                           wring[:, blk % RING, k, :], k == 0, False)
                    mm(ps[:, b, 0:WCOLS], ones[0:1, :], bias_row[:, WCOLS * m:WCOLS * (m + 1)],
                       False, True)
                    for k in range(KP):
                        ins = mm(ps[:, b, WCOLS:2 * WCOLS], pT[:, k, P * i:P * (i + 1)],
                                 w_proj[:, k, WCOLS * m:WCOLS * (m + 1)], k == 0, k == KP - 1)
                    ins.then_inc(ple_mm, 1)

                def add_rows(step, tile, half):
                    for r in range(G):
                        pe.wait_ge(v_loaded[r], (step * 2 + half + 1) * 16)
                        pe.wait_ge(diag_ready, step * TOPK + half * G + r + 1)
                        for m in range(2):
                            ins = mm(bank(2 * tile + m), diag[:, r, :],
                                     vrow[:, r, BANK * m:BANK * (m + 1)], False, False)
                        ins.then_inc(v_free, 1)

                for step in range(NSTEP):
                    add_rows(step, step // HP, 0)
                    if step + AHEAD < HP:
                        queries(step + AHEAD)
                    add_rows(step, step // HP, 1)
                    if step + AHEAD < HP:
                        score(step + AHEAD)
                    for i, m in behind.get(step, ()):
                        embed(i, m)
                meet(pe, layer)


_INS = ["x_prompt", "x_sample", "state_gla", "state_gdn", "state_conv", "p_prompt", "p_sample",
        "norm_mix", "w_in", "w_gla_up", "b_gla_gate", "gla_norm", "conv_w", "gdn_a_log",
        "gdn_dt_bias", "gdn_norm", "w_out", "norm_ffn", "w_peer_q", "peer_sub_keys", "peer_u",
        "peer_v", "norm_ple", "w_ple_gate", "b_ple_gate", "w_ple_proj", "norm_final"]


def _outs(i):
    shape = {k: tuple(v.shape) for k, v in i.items()}
    depth, batch = shape["state_gla"][0], shape["x_prompt"][0]
    out = [shape["x_prompt"], shape["x_sample"]]
    for n in (batch, None):
        for s in ("state_gla", "state_gdn", "state_conv"):
            rest = shape[s][2:]
            out.append((depth, n if n is not None else shape[s][1]) + rest)
    return out


def kernel(**inputs):
    import numpy as _np
    import concourse.bacc as _bacc
    from concourse import mybir as _mybir
    from concourse.bass_utils import run_bass_kernel_spmd as _run

    nc = _bacc.Bacc("TRN2", target_bir_lowering=False, num_devices=1)
    arrays, args = {}, []
    for name in _INS:
        a = _np.ascontiguousarray(inputs[name])
        arrays[f"in_{name}_dram"] = a
        args.append(nc.dram_tensor(f"in_{name}_dram", a.shape, _mybir.dt.from_np(a.dtype),
                                   kind="ExternalInput").ap())
    shapes = _outs(inputs)
    for i, shape in enumerate(shapes):
        args.append(nc.dram_tensor(f"out_{i}_dram", shape, _mybir.dt.float32,
                                   kind="ExternalOutput").ap())
    hybrid_trunk(nc, *args)
    r = _run(nc, [arrays], core_ids=[0])
    return tuple(r.results[0][f"out_{i}_dram"] for i in range(len(shapes)))
```
